# Optimizing a Trainium2 kernel written in Bass

```python
import jax, jax.numpy as jnp
from jax import lax
import numpy as np

D_MODEL = 1024
BATCH = 1
SEQ = 1024
DEPTH = 1

NSA_HEADS = 8
NSA_KV_GROUPS = 2
NSA_HEAD_DIM = 64
NSA_WIDTH = NSA_HEADS * NSA_HEAD_DIM
NSA_BRANCHES = 3
CMP_STRIDE = 16
CMP_LEN = 2 * CMP_STRIDE
CMP_HIDDEN = 256
SEL_BLOCK = 64
SEL_TOPN = 16
SEL_QCHUNK = 64
WINDOW = 512
WIN_QBLOCK = 128

HGRN_WIDTH = D_MODEL - NSA_WIDTH
HGRN_EXPAND = 128
HGRN_HEADS = HGRN_WIDTH // HGRN_EXPAND
HGRN_DK = HGRN_EXPAND
HGRN_DV = HGRN_WIDTH // HGRN_HEADS
HGRN_CHUNK = 64

MIX_WIDTH = NSA_WIDTH + HGRN_WIDTH

MOE_GROUPS = 4
EXPERTS_PER_GROUP = 8
N_EXPERTS = MOE_GROUPS * EXPERTS_PER_GROUP
MOE_TOPK = 2
EXPERT_FF = 512
MOE_BLOCK = 256

RMS_EPS = 1e-6
NEG_INF = -1e30

KV_DIM = NSA_KV_GROUPS * NSA_HEAD_DIM
IN_SPLITS = (NSA_WIDTH,) + (KV_DIM,) * (2 * NSA_BRANCHES) + (NSA_HEADS * NSA_BRANCHES,) + (HGRN_WIDTH,) * 4
IN_COLS = sum(IN_SPLITS)

kernel_name = 'hybrid_nsa_hgrn2_hmoe'

def rmsnorm(x, g):
    xf = x.astype(jnp.float32)
    y = xf * lax.rsqrt(jnp.mean(xf * xf, axis=-1, keepdims=True) + RMS_EPS)
    return (y * g.astype(jnp.float32)).astype(x.dtype)

def nsa_mixer(q, kc_raw, vc_raw, ks_raw, vs_raw, kw_raw, vw_raw, gate_logits,
              g_q, g_k, pos_k, pos_v, wk1, wk2, wv1, wv2):
    B, S = q.shape[0], q.shape[1]
    G, R, DH = NSA_KV_GROUPS, NSA_HEADS // NSA_KV_GROUPS, NSA_HEAD_DIM
    dt = q.dtype
    scale = DH ** -0.5
    qn = rmsnorm(q, g_q).reshape(B, S, G, R, DH).transpose(0, 2, 3, 1, 4)
    t_pos = jnp.arange(S)

    def to_groups(t):
        return t.reshape(B, S, G, DH).transpose(0, 2, 1, 3)

    nc = S // CMP_STRIDE - 1

    def compress(t, pos, w1, w2):
        ch = to_groups(t).reshape(B, G, S // CMP_STRIDE, CMP_STRIDE, DH)
        blk = jnp.concatenate([ch[:, :, :-1], ch[:, :, 1:]], axis=3) + pos
        hid = jax.nn.silu(blk.reshape(B, G, nc, CMP_LEN * DH) @ w1)
        return hid @ w2

    kc = rmsnorm(compress(kc_raw, pos_k, wk1, wk2), g_k[0])
    vc = compress(vc_raw, pos_v, wv1, wv2)
    s_c = jnp.einsum('bgrsd,bgcd->bgrsc', qn, kc).astype(jnp.float32) * scale
    mask_c = (jnp.arange(nc) * CMP_STRIDE + CMP_LEN - 1)[None, :] <= t_pos[:, None]
    p_c = jax.nn.softmax(jnp.where(mask_c, s_c, NEG_INF), axis=-1) * mask_c
    o_c = jnp.einsum('bgrsc,bgcd->bgrsd', p_c.astype(dt), vc)

    ns = S // SEL_BLOCK
    top_n = min(SEL_TOPN, ns)
    cs = np.arange(nc)[:, None] * CMP_STRIDE
    js = np.arange(ns)[None, :] * SEL_BLOCK
    overlap = np.clip(np.minimum(cs + CMP_LEN, js + SEL_BLOCK) - np.maximum(cs, js), 0, None)
    overlap = jnp.asarray(overlap / CMP_LEN, dtype=jnp.float32)
    imp = jnp.einsum('bgrsc,cj->bgsj', p_c, overlap)
    cur_blk = t_pos // SEL_BLOCK
    jb = jnp.arange(ns)
    valid = jb[None, :] <= cur_blk[:, None]
    forced = (jb[None, :] == cur_blk[:, None]) | (jb[None, :] == 0)
    imp = jnp.where(forced, jnp.inf, jnp.where(valid, imp, -jnp.inf))
    _, sel_idx = lax.top_k(imp, top_n)

    ks_blk = rmsnorm(to_groups(ks_raw), g_k[1]).reshape(B, G, ns, SEL_BLOCK, DH)
    vs_blk = to_groups(vs_raw).reshape(B, G, ns, SEL_BLOCK, DH)
    nqc = S // SEL_QCHUNK
    q_ch = qn.reshape(B, G, R, nqc, SEL_QCHUNK, DH).transpose(3, 0, 1, 2, 4, 5)
    i_ch = sel_idx.reshape(B, G, nqc, SEL_QCHUNK, top_n).transpose(2, 0, 1, 3, 4)
    gather = jax.vmap(jax.vmap(lambda blocks, ix: blocks[ix]))
    n_keys = top_n * SEL_BLOCK

    def sel_chunk(args):
        qb, ib, ci = args
        kg = gather(ks_blk, ib).reshape(B, G, SEL_QCHUNK, n_keys, DH)
        vg = gather(vs_blk, ib).reshape(B, G, SEL_QCHUNK, n_keys, DH)
        kpos = (ib[..., None] * SEL_BLOCK + jnp.arange(SEL_BLOCK)).reshape(B, G, SEL_QCHUNK, n_keys)
        tq = ci * SEL_QCHUNK + jnp.arange(SEL_QCHUNK)
        m = kpos <= tq[None, None, :, None]
        s = jnp.einsum('bgrqd,bgqkd->bgrqk', qb, kg).astype(jnp.float32) * scale
        p = jax.nn.softmax(jnp.where(m[:, :, None], s, NEG_INF), axis=-1)
        return jnp.einsum('bgrqk,bgqkd->bgrqd', p.astype(dt), vg)

    o_s = lax.map(sel_chunk, (q_ch, i_ch, jnp.arange(nqc)))
    o_s = o_s.transpose(1, 2, 3, 0, 4, 5).reshape(B, G, R, S, DH)

    nqb = S // WIN_QBLOCK
    n_band = WINDOW // WIN_QBLOCK + 1
    band = n_band * WIN_QBLOCK

    def banded(t):
        tp = jnp.pad(t, ((0, 0), (0, 0), (WINDOW, 0), (0, 0)))
        tp = tp.reshape(B, G, (S + WINDOW) // WIN_QBLOCK, WIN_QBLOCK, DH)
        bands = jnp.concatenate([tp[:, :, i:i + nqb] for i in range(n_band)], axis=3)
        return bands.transpose(2, 0, 1, 3, 4)

    kw_band = banded(rmsnorm(to_groups(kw_raw), g_k[2]))
    vw_band = banded(to_groups(vw_raw))
    qi = jnp.arange(WIN_QBLOCK)[:, None]
    mi = jnp.arange(band)[None, :]
    rel_ok = (mi >= qi + 1) & (mi <= qi + WINDOW)
    pos_ok = (jnp.arange(nqb)[:, None] * WIN_QBLOCK - WINDOW + jnp.arange(band)[None, :]) >= 0
    mask_w = rel_ok[None] & pos_ok[:, None, :]
    q_wb = qn.reshape(B, G, R, nqb, WIN_QBLOCK, DH).transpose(3, 0, 1, 2, 4, 5)

    def win_block(args):
        qb, kb, vb, mb = args
        s = jnp.einsum('bgrqd,bgkd->bgrqk', qb, kb).astype(jnp.float32) * scale
        p = jax.nn.softmax(jnp.where(mb, s, NEG_INF), axis=-1)
        return jnp.einsum('bgrqk,bgkd->bgrqd', p.astype(dt), vb)

    o_w = lax.map(win_block, (q_wb, kw_band, vw_band, mask_w))
    o_w = o_w.transpose(1, 2, 3, 0, 4, 5).reshape(B, G, R, S, DH)

    gates = jax.nn.sigmoid(gate_logits.astype(jnp.float32)).astype(dt)
    gates = gates.reshape(B, S, G, R, NSA_BRANCHES).transpose(4, 0, 2, 3, 1)[..., None]
    o = gates[0] * o_c + gates[1] * o_s + gates[2] * o_w
    return o.transpose(0, 3, 1, 2, 4).reshape(B, S, NSA_WIDTH)

def hgrn2_mixer(q, f, i, g, lb, g_norm):
    B, S = q.shape[0], q.shape[1]
    H, K, V, C = HGRN_HEADS, HGRN_DK, HGRN_DV, HGRN_CHUNK
    dt = q.dtype

    def heads(t, d):
        return t.reshape(B, S, H, d).transpose(0, 2, 1, 3).astype(jnp.float32)

    lbh = lb.astype(jnp.float32).reshape(H, 1, K)
    qf = jax.nn.silu(heads(q, K))
    fg = lbh + (1.0 - lbh) * jax.nn.sigmoid(heads(f, K))
    kf = 1.0 - fg
    logf = jnp.log(fg)
    vf = heads(i, V)
    nch = S // C

    def chunk(t):
        return t.reshape(B, H, nch, C, t.shape[-1]).transpose(2, 0, 1, 3, 4)

    causal = jnp.tril(jnp.ones((C, C), dtype=bool))[:, :, None]

    def step(state, xs):
        qc, kc, vc, lc = xs
        a = jnp.cumsum(lc, axis=2)
        decay = jnp.exp(jnp.where(causal, a[:, :, :, None, :] - a[:, :, None, :, :], -jnp.inf))
        attn = jnp.einsum('bhtk,bhsk,bhtsk->bhts', qc, kc, decay)
        out = attn @ vc + jnp.einsum('bhtk,bhkv->bhtv', qc * jnp.exp(a), state)
        a_last = a[:, :, -1:, :]
        new_state = jnp.exp(a_last[:, :, 0, :, None]) * state + jnp.einsum('bhsk,bhsv->bhkv', kc * jnp.exp(a_last - a), vc)
        return new_state, out

    _, o = lax.scan(step, jnp.zeros((B, H, K, V), jnp.float32), (chunk(qf), chunk(kf), chunk(vf), chunk(logf)))
    o = o.transpose(1, 3, 0, 2, 4).reshape(B, S // C * 0 + nch, C, H, V) if False else o.transpose(1, 0, 3, 2, 4).reshape(B, S, H, V)
    o = rmsnorm(o, g_norm).reshape(B, S, HGRN_WIDTH) * jax.nn.silu(g.astype(jnp.float32))
    return o.astype(dt)

def hier_moe(x, w_group, b_group, w_expert, b_expert, w1, w3, w2):
    B, S, D = x.shape
    N = B * S
    xt = x.reshape(N, D)
    pg = jax.nn.softmax((xt @ w_group).astype(jnp.float32) + b_group.astype(jnp.float32), axis=-1)
    pg_top, g_idx = lax.top_k(pg, 1)
    le = ((xt @ w_expert).astype(jnp.float32) + b_expert.astype(jnp.float32)).reshape(N, MOE_GROUPS, EXPERTS_PER_GROUP)
    le = jnp.take_along_axis(le, jnp.broadcast_to(g_idx[:, :, None], (N, 1, EXPERTS_PER_GROUP)), axis=1)[:, 0]
    pe = jax.nn.softmax(le, axis=-1)
    pe_top, e_loc = lax.top_k(pe, MOE_TOPK)
    w_tok = pg_top * pe_top / jnp.sum(pe_top, axis=-1, keepdims=True)
    e_id = g_idx * EXPERTS_PER_GROUP + e_loc

    n_asg = N * MOE_TOPK
    e_flat = e_id.reshape(n_asg)
    w_flat = w_tok.reshape(n_asg)
    tok = jnp.repeat(jnp.arange(N), MOE_TOPK)
    order = jnp.argsort(e_flat)
    e_s, tok_s, w_s = e_flat[order], tok[order], w_flat[order]
    counts = jnp.bincount(e_flat, length=N_EXPERTS)
    start = jnp.cumsum(counts) - counts
    padded = (counts + MOE_BLOCK - 1) // MOE_BLOCK * MOE_BLOCK
    pend = jnp.cumsum(padded)
    pstart = pend - padded
    dest = pstart[e_s] + jnp.arange(n_asg) - start[e_s]
    P = n_asg + N_EXPERTS * MOE_BLOCK
    nblk = P // MOE_BLOCK
    x_pad = jnp.zeros((P, D), x.dtype).at[dest].set(xt[tok_s])
    blk_e = jnp.minimum(jnp.sum(jnp.arange(nblk)[:, None] * MOE_BLOCK >= pend[None, :], axis=1), N_EXPERTS - 1)

    def expert_block(args):
        xb, e = args
        return (jax.nn.silu(xb @ w1[e]) * (xb @ w3[e])) @ w2[e]

    y_pad = lax.map(expert_block, (x_pad.reshape(nblk, MOE_BLOCK, D), blk_e)).reshape(P, D)
    y = jax.ops.segment_sum(y_pad[dest] * w_s[:, None].astype(x.dtype), tok_s, num_segments=N)
    return y.reshape(B, S, D)

def setup_inputs(seed: int = 0) -> dict:
    key = jax.random.key(seed)
    ks = jax.random.split(key, 24)
    nrm = lambda k, shape, s: jax.random.normal(k, shape, jnp.float32) * s
    DH = NSA_HEAD_DIM
    return {
        'x': nrm(ks[0], (BATCH, SEQ, D_MODEL), 1.0),
        'attn_norm_g': 1.0 + nrm(ks[1], (DEPTH, D_MODEL), 0.02),
        'ffn_norm_g': 1.0 + nrm(ks[2], (DEPTH, D_MODEL), 0.02),
        'w_in': nrm(ks[3], (DEPTH, D_MODEL, IN_COLS), D_MODEL ** -0.5),
        'w_out': nrm(ks[4], (DEPTH, MIX_WIDTH, D_MODEL), MIX_WIDTH ** -0.5),
        'nsa_q_norm_g': 1.0 + nrm(ks[5], (DEPTH, DH), 0.02),
        'nsa_k_norm_g': 1.0 + nrm(ks[6], (DEPTH, NSA_BRANCHES, DH), 0.02),
        'cmp_pos_k': nrm(ks[7], (DEPTH, CMP_LEN, DH), 0.1),
        'cmp_pos_v': nrm(ks[8], (DEPTH, CMP_LEN, DH), 0.1),
        'cmp_wk1': nrm(ks[9], (DEPTH, CMP_LEN * DH, CMP_HIDDEN), (CMP_LEN * DH) ** -0.5),
        'cmp_wk2': nrm(ks[10], (DEPTH, CMP_HIDDEN, DH), CMP_HIDDEN ** -0.5),
        'cmp_wv1': nrm(ks[11], (DEPTH, CMP_LEN * DH, CMP_HIDDEN), (CMP_LEN * DH) ** -0.5),
        'cmp_wv2': nrm(ks[12], (DEPTH, CMP_HIDDEN, DH), CMP_HIDDEN ** -0.5),
        'nsa_out_norm_g': 1.0 + nrm(ks[13], (DEPTH, NSA_WIDTH), 0.02),
        'hgrn_lb_logits': nrm(ks[14], (DEPTH + 1, HGRN_WIDTH), 0.5),
        'hgrn_out_norm_g': 1.0 + nrm(ks[15], (DEPTH, HGRN_DV), 0.02),
        'moe_w_group': nrm(ks[16], (DEPTH, D_MODEL, MOE_GROUPS), D_MODEL ** -0.5),
        'moe_b_group': nrm(ks[17], (DEPTH, MOE_GROUPS), 0.01),
        'moe_w_expert': nrm(ks[18], (DEPTH, D_MODEL, N_EXPERTS), D_MODEL ** -0.5),
        'moe_b_expert': nrm(ks[19], (DEPTH, N_EXPERTS), 0.01),
        'moe_w1': nrm(ks[20], (DEPTH, N_EXPERTS, D_MODEL, EXPERT_FF), D_MODEL ** -0.5),
        'moe_w3': nrm(ks[21], (DEPTH, N_EXPERTS, D_MODEL, EXPERT_FF), D_MODEL ** -0.5),
        'moe_w2': nrm(ks[22], (DEPTH, N_EXPERTS, EXPERT_FF, D_MODEL), EXPERT_FF ** -0.5),
    }

def reference(x, attn_norm_g, ffn_norm_g, w_in, w_out, nsa_q_norm_g, nsa_k_norm_g,
              cmp_pos_k, cmp_pos_v, cmp_wk1, cmp_wk2, cmp_wv1, cmp_wv2, nsa_out_norm_g,
              hgrn_lb_logits, hgrn_out_norm_g, moe_w_group, moe_b_group, moe_w_expert,
              moe_b_expert, moe_w1, moe_w3, moe_w2):
    B, S, _ = x.shape
    split_at = np.cumsum(IN_SPLITS)[:-1].tolist()
    lb_all = jnp.cumsum(jax.nn.softmax(hgrn_lb_logits.astype(jnp.float32), axis=0), axis=0)
    h = x
    for layer in range(DEPTH):
        n = rmsnorm(h, attn_norm_g[layer])
        parts = jnp.split(n @ w_in[layer], split_at, axis=-1)
        q = parts[0].reshape(B, S, NSA_HEADS, NSA_HEAD_DIM)
        gate_logits = parts[7].reshape(B, S, NSA_HEADS, NSA_BRANCHES)
        o_nsa = nsa_mixer(q, parts[1], parts[2], parts[3], parts[4], parts[5], parts[6], gate_logits,
                          nsa_q_norm_g[layer], nsa_k_norm_g[layer], cmp_pos_k[layer], cmp_pos_v[layer],
                          cmp_wk1[layer], cmp_wk2[layer], cmp_wv1[layer], cmp_wv2[layer])
        o_nsa = rmsnorm(o_nsa, nsa_out_norm_g[layer])
        o_hgrn = hgrn2_mixer(parts[8], parts[9], parts[10], parts[11], lb_all[layer], hgrn_out_norm_g[layer])
        mixed = jnp.concatenate([o_nsa, o_hgrn.astype(o_nsa.dtype)], axis=-1)
        h = h + mixed @ w_out[layer]
        h = h + hier_moe(rmsnorm(h, ffn_norm_g[layer]), moe_w_group[layer], moe_b_group[layer],
                         moe_w_expert[layer], moe_b_expert[layer], moe_w1[layer], moe_w3[layer], moe_w2[layer])
    return h


_drawn_inputs = setup_inputs


def setup_inputs(seed=0):
    import zlib

    import numpy as np

    out = dict(_drawn_inputs(seed))
    spreads = {}
    factors = {'nsa_q_norm_g': 3.382,
     'nsa_k_norm_g': 3.857,
     'nsa_out_norm_g': 9.694,
     'hgrn_out_norm_g': 14.309,
     'moe_b_group': 29.878,
     'moe_b_expert': 21.339,
     'ffn_norm_g': 5.995}
    for name, (base, spread) in spreads.items():
        noise = np.random.default_rng([zlib.crc32(name.encode()), seed]).standard_normal(out[name].shape)
        drawn = base * np.exp(spread * noise) if base else spread * noise
        out[name] = __import__('jax').numpy.asarray(drawn.astype(out[name].dtype))
    for name, factor in factors.items():
        out[name] = (out[name] * factor).astype(out[name].dtype)
    return out
```

```python
from contextlib import ExitStack

import concourse.bass as bass
from concourse import mybir
from concourse.alu_op_type import AluOpType as ALU

F32 = mybir.dt.float32
I32 = mybir.dt.int32
U32 = mybir.dt.uint32
U8 = mybir.dt.uint8
ACT = mybir.ActivationFunctionType
AX = mybir.AxisListType

P = 128
S = 1024
D = 1024
NT = S // P
KT = D // P
HALF = 512
EPS = 1e-6
NEG = -1e30

HEADS, GROUPS, DH = 8, 2, 64
REP = HEADS // GROUPS
PAIRS = REP // 2
NSA_W = HEADS * DH
CSTR, CLEN, CHID = 16, 32, 256
NC = S // CSTR - 1
CM = CLEN // 2
WINDOW = 512
HH, DK = 4, 128
HG_W = HH * DK
KV = GROUPS * DH
C_Q, C_KC, C_VC, C_KS, C_VS, C_KW, C_VW = [0] + [NSA_W + i * KV for i in range(6)]
C_GATE = NSA_W + 6 * KV
C_HQ = C_GATE + 3 * HEADS
C_HF, C_HI, C_HG = C_HQ + HG_W, C_HQ + 2 * HG_W, C_HQ + 3 * HG_W
IN_COLS = C_HQ + 4 * HG_W
LEVELS = 7

NG, EPG, NE, FF = 4, 8, 32, 512
BLK = 64
MAXBLK = S * 2 // BLK + NE
SLOTS = MAXBLK * BLK
FT = FF // P


class Chain:

    def __init__(self, eng, sem, per_round=0):
        self.eng, self.sem, self.per_round, self.base, self.n = eng, sem, per_round, 0, 0

    def round(self, i):
        self.base, self.n = i * self.per_round, 0

    def __call__(self, ins):
        self.n += 1
        ins.then_inc(self.sem, 1)

    def wait(self):
        self.eng.wait_ge(self.sem, self.base + self.n)

    def link(self, ins):
        self(ins)
        self.wait()

    def end(self):
        assert self.n == self.per_round, (self.n, self.per_round)


class Core:

    def __init__(self, nc, ctx):
        self.nc, self.ctx = nc, ctx

    def sb(self, name, shape, off, dt=F32):
        return self.nc.alloc_sbuf_tensor_at(name, shape, dt, offset=SB_BASE + off)

    def sem(self, name):
        return self.ctx.enter_context(self.nc.semaphore(name))

    def sems(self, prefix, names):
        return {n: self.sem(prefix + n) for n in names}


class Constants:
    pass


class Map:

    def __init__(self, core, at, end):
        self.core, self.at, self.last = core, at, end

    def __call__(self, name, shape, dt=F32):
        n = {F32: 4, I32: 4, U32: 4, U8: 1}[dt]
        for s in shape[1:]:
            n *= s
        t = self.core.sb(name, shape, self.at, dt)
        self.at += (n + 31) // 32 * 32
        assert self.at <= self.last, (name, self.at, self.last)
        return t


KB = 1024
SB_BASE = 16 * KB + 128
R_CONST = (0, 16 * KB)
R_X = (16 * KB, 48 * KB)
R_MIX = (48 * KB, 80 * KB)
R_NT = (80 * KB, 112 * KB)
R_WORK = (112 * KB, 207 * KB)


def constants(core):
    c = Map(core, *R_CONST)
    k = core.k
    k.ident = c("ident", [P, P])
    k.ones = c("ones", [P, P])
    k.halves = c("halves", [P, P])
    k.before = c("before", [P, P])
    k.causal = c("causal", [P, P])
    k.far = c("far", [P, P])
    k.cmask = c("cmask", [P, NT, NC + 1])
    k.cneg = c("cneg", [P, NT, NC + 1])
    k.lmask = c("lmask", [P, LEVELS, P], U8)
    k.lmaskf = core.sb("lmaskf", [P, LEVELS, P], R_MIX[0])
    k.reset = c("reset", [P, S])
    k.eps = c("eps", [P, 1])
    k.g_hg = c("g_hg", [P, DK])
    k.g_attn = c("g_attn", [P, KT])
    k.g_nsa = c("g_nsa", [P, NSA_W // P])
    k.gq = c("gq", [P, 1])
    k.gkk = c("gkk", [P, 1])
    k.gkc = c("gkc", [P, 1])
    k.lb = c("lb", [P, HH])
    k.oml = c("oml", [P, HH])
    k.lbl = c("lbl", [P, 2, HH])
    k.brt = c("brt", [P, NG + NE])
    k.order = c("order", [P, NE])
    k.wr = c("wr", [P, KT, NG + NE])


def first_norm(nc, core, a):
    k = core.k
    xt, nT = core.xt, core.nT
    x_in = core.x_in
    w = Map(core, R_MIX[0] + 8 * KB, R_MIX[1])
    sq = w("n_sq", [P, D])
    ss = w("n_ss", [P, 4, 2])
    pt = core.pt
    x_sum, x_rs, x_nrm, x_T, x_ev, x_free, c_a = (core.sem(n) for n in (
        "n_sum", "n_rs", "n_scaled", "n_turned", "n_out", "n_free", "n_act"))
    s_ms, s_sel, s_in, g_in, s_a, s_v = (core.sem(n) for n in (
        "const_filled", "const_shaped", "const_in", "gain_in", "const_act", "const_dve"))
    U = 4
    with nc.Block() as block:

        @block.sync
        def _(sp):
            loads = [
                (k.g_nsa[:], a["nsa_out_norm_g"].rearrange("o (t p) -> p (o t)", p=P)),
                (k.gq[0:DH], a["nsa_q_norm_g"].rearrange("o d -> d o")),
                (k.gq[DH:P], a["nsa_q_norm_g"].rearrange("o d -> d o")),
                (k.gkc[0:DH], a["nsa_k_norm_g"][0, 0:1].rearrange("o d -> d o")),
                (k.gkc[DH:P], a["nsa_k_norm_g"][0, 0:1].rearrange("o d -> d o")),
                (k.gkk[0:DH], a["nsa_k_norm_g"][0, 1:2].rearrange("o d -> d o")),
                (k.gkk[DH:P], a["nsa_k_norm_g"][0, 2:3].rearrange("o d -> d o")),
                (k.lbl[:, 0], a["hgrn_lb_logits"][0].rearrange("(h p) -> p h", p=P)),
                (k.lbl[:, 1], a["hgrn_lb_logits"][1].rearrange("(h p) -> p h", p=P)),
                (k.g_hg[:], a["hgrn_out_norm_g"][0].partition_broadcast(P)),
                (k.brt[:, 0:NG], a["moe_b_group"][0].partition_broadcast(P)),
                (k.brt[:, NG:NG + NE], a["moe_b_expert"][0].partition_broadcast(P)),
                (k.wr[:, :, 0:NG], a["moe_w_group"][0].rearrange("(t p) n -> p t n", p=P)),
                (k.wr[:, :, NG:NG + NE], a["moe_w_expert"][0].rearrange("(t p) n -> p t n", p=P)),
            ]
            for u in range(U):
                sp.dma_start(xt[:, u], a["x"][0, u * P:(u + 1) * P]).then_inc(x_in[u], 16)
            with nc.allow_non_contiguous_dma(reason="gains and biases, a few bytes each"):
                sp.dma_start(k.g_attn[:], a["attn_norm_g"].rearrange("o (t p) -> p (o t)", p=P)).then_inc(g_in, 16)
            load_head(sp, core, a, 0)
            for u in range(U):
                sp.wait_ge(x_T, u + 1)
                sp.dma_start(xt[:, u], a["x"][0, (U + u) * P:(U + u + 1) * P]).then_inc(x_in[u], 16)
            with nc.allow_non_contiguous_dma(reason="gains and biases, a few bytes each"):
                for out, src in loads:
                    sp.dma_start(out, src).then_inc(s_in, 16)
            sp.wait_ge(s_in, 16 * len(loads))

        @block.gpsimd
        def _(g):
            sel = []

            def select(out, pattern, op, fill, base, cm):
                if sel:
                    g.wait_ge(s_sel, len(sel))
                sel.append(g.affine_select(out=out, in_=out, pattern=pattern, compare_op=op, fill=fill,
                                           base=base, channel_multiplier=cm).then_inc(s_sel, 1))

            g.memset(k.ident[:], 0.0).then_inc(s_ms, 1)
            g.memset(k.eps[:], EPS).then_inc(s_ms, 1)
            g.wait_ge(s_ms, 2)
            select(k.ident[:], [[-1, P]], ALU.not_equal, 1.0, 0, 1)
            n = 2
            for t, v in ((k.ones, 1.0), (k.halves, 1.0 / DH), (k.before, 1.0),
                         (k.causal, 0.0), (k.far, 0.0), (k.cmask, 1.0), (k.cneg, 0.0),
                         (k.lmaskf, 1.0), (k.reset, 1.0)):
                g.memset(t[:], v).then_inc(s_ms, 1)
                n += 1
            g.wait_ge(s_ms, n)
            select(k.halves[0:DH, DH:P], [[0, DH]], ALU.is_gt, 0.0, 0, 0)
            select(k.halves[DH:P, 0:DH], [[0, DH]], ALU.is_gt, 0.0, 0, 0)
            select(k.before[:], [[1, P]], ALU.is_gt, 0.0, 0, -1)
            select(k.causal[:], [[-1, P]], ALU.is_ge, NEG, 0, 1)
            select(k.far[:], [[1, P]], ALU.is_gt, NEG, 0, -1)
            select(k.cmask[:], [[P, NT], [-CSTR, NC + 1]], ALU.is_ge, 0.0, 1 - CLEN, 1)
            select(k.cneg[:], [[P, NT], [-CSTR, NC + 1]], ALU.is_ge, NEG, 1 - CLEN, 1)
            select(k.reset[:].rearrange("p (c t) -> p c t", t=P), [[0, NT], [1, P]], ALU.is_gt, 0.0, 0, 0)
            for l in range(LEVELS):
                B = 1 << l
                n_blk = P // (2 * B)
                m = k.lmaskf[:, l].rearrange("p (n two b) -> p n two b", two=2, b=B)
                select(m[:, :, 0], [[0, n_blk], [0, B]], ALU.is_gt, 0.0, 0, 0)
                select(m[:, :, 1], [[-2 * B, n_blk], [0, B]], ALU.is_ge, 0.0, 0, 1)
                select(m[:, :, 1], [[2 * B, n_blk], [0, B]], ALU.is_gt, 0.0, B, -1)
            g.wait_ge(s_sel, len(sel))
            g.tensor_copy(k.lmask[:], k.lmaskf[:]).then_inc(s_sel, 1)
            g.wait_ge(s_sel, len(sel) + 1)
            g.iota(k.order[:], pattern=[[-1, NE]], base=NE, channel_multiplier=0,
                   allow_small_or_imprecise_dtypes=True).then_inc(s_sel, 1)
            g.wait_ge(s_sel, len(sel) + 2)

        @block.scalar
        def _(act):
            act.preload_act_table_set("natural_log_exp_and_others")
            c = Chain(act, c_a, 2 * U)
            act.wait_ge(s_ms, 2)
            with act.Fori(0, NT // U) as i:
                c.round(i)
                for u in range(U):
                    act.wait_ge(x_in[u], i * 16 + 16)
                    c.link(nc.scalar.activation(sq[:], xt[:, u], ACT.Square, accum_out=ss[:, u, 0:1]))
                    c.link(nc.scalar.activation(ss[:, u, 0:1], ss[:, u, 0:1], ACT.Ln, scale=1.0 / D, bias=k.eps[:]))
                    nc.scalar.activation(ss[:, u, 1:2], ss[:, u, 0:1], ACT.Exp, scale=-0.5).then_inc(x_rs, 1)
                c.end()
            act.wait_ge(s_v, 3)
            nc.scalar.activation(k.lbl[:], k.lbl[:], ACT.Exp).then_inc(s_a, 1)

        @block.vector
        def _(dve):
            dve.wait_ge(g_in, 16)
            with dve.Fori(0, NT // U) as i:
                for u in range(U):
                    dve.wait_ge(x_rs, i * U + u + 1)
                    nc.vector.tensor_scalar(xt[:, u], xt[:, u], ss[:, u, 1:2], None, ALU.mult).then_inc(x_nrm, 1)
                    dve.wait_ge(x_T, i * U + u + 1)
                    p = pt[u % 2]
                    nc.vector.tensor_tensor(nT[:, :, bass.ts(i * U + u, P)], p[:].rearrange("p (k t) -> p k t", t=P),
                                            k.g_attn[:].unsqueeze(2).to_broadcast([P, KT, P]),
                                            ALU.mult).then_inc(x_ev, 1)
            c = Chain(dve, s_v)
            dve.wait_ge(s_in, 16 * 14)
            c.link(nc.vector.tensor_max(k.lb[:], k.lbl[:, 0], k.lbl[:, 1]))
            c.link(nc.vector.tensor_sub(k.lbl[:, 0], k.lbl[:, 0], k.lb[:]))
            c.link(nc.vector.tensor_sub(k.lbl[:, 1], k.lbl[:, 1], k.lb[:]))
            dve.wait_ge(s_a, 1)
            c.link(nc.vector.tensor_add(k.oml[:], k.lbl[:, 0], k.lbl[:, 1]))
            c.link(nc.vector.reciprocal(k.oml[:], k.oml[:]))
            c.link(nc.vector.tensor_mul(k.lb[:], k.lbl[:, 0], k.oml[:]))
            c.link(nc.vector.tensor_mul(k.oml[:], k.lbl[:, 1], k.oml[:]))

        @block.tensor
        def _(pe):
            pe.sem_inc(x_ev, 2)
            pe.wait_ge(s_sel, 1)
            with pe.Fori(0, NT // U) as i:
                for u in range(U):
                    pe.wait_ge(x_nrm, i * U + u + 1)
                    pe.wait_ge(x_ev, i * U + u + 1)
                    for kt in range(KT):
                        last = nc.tensor.transpose(pt[u % 2][:, kt * P:(kt + 1) * P], xt[:, u, kt * P:(kt + 1) * P],
                                                   k.ident[:])
                    last.then_inc(x_T, 1)


def load_head(sp, core, a, i):
    win = a["w_in"][0].rearrange("(t p) n -> p t n", p=P)
    if not isinstance(i, int):
        sp.wait_ge(core.wt_free, i)
    for j, col in ((0, C_HQ), (1, C_HF)):
        sp.dma_start(core.wt[:, j], win[:, :, bass.ds(col + i * DK, DK)]).then_inc(core.wt_in, 16)
    if not isinstance(i, int):
        sp.wait_ge(core.ww_free, i)
    for j, col in ((0, C_HI), (1, C_HG)):
        sp.dma_start(core.ww[:, :, j * DK:(j + 1) * DK], win[:, :, bass.ds(col + i * DK, DK)]).then_inc(core.ww_in, 16)


def hgrn(nc, core, a):
    k, nT, mixed, ps = core.k, core.nT, core.mixed, core.ps
    w = Map(core, *R_WORK)
    zero = core.sb("h_zero", [BLK, D], 203 * KB)
    wt, ww = core.wt, core.ww
    w.at = core.wtw_end
    e1 = w("h_e1", [P, S])
    e2 = w("h_e2", [P, S])
    fg = w("h_fg", [P, S])
    lf = w("h_lf", [P, S])
    cum = w("h_cum", [P, S])
    q = w("h_q", [P, S])
    kf = w("h_kf", [P, S])
    qh = w("h_qh", [P, S])
    kh = w("h_kh", [P, S])
    x = Map(core, *R_X)
    dd = [x("h_d0", [P, S]), x("h_d1", [P, S])]
    qe = [x("h_qe0", [P, S]), x("h_qe1", [P, S])]
    ke = [x("h_ke0", [P, S]), x("h_ke1", [P, S])]
    dec = x("h_dec", [P, NT])
    ssq = x("h_ssq", [P, 2, NT])
    vg = w("h_vg", [P, NT, 2 * DK])
    at = w("h_at", [P, NT, P])
    kt_sb = w("h_kt", [P, NT, P])
    st = w("h_st", [P, NT, P])
    og = w("h_og", [P, NT, P])
    gg = w("h_gg", [P, NT, DK])
    TQ, TF = ps[:, 0:2 * HALF], ps[:, 2 * HALF:4 * HALF]
    U, O = TQ, TF
    TOK = [ps[:, 4 * HALF:4 * HALF + 2 * DK], ps[:, 5 * HALF:5 * HALF + 2 * DK]]
    LV = [ps[:, 6 * HALF:7 * HALF], ps[:, 7 * HALF:8 * HALF]]
    names = ("f_ready q_ready u_free o_free tok_ready tok_out mix_done ef eq "
             "fg lf d_ready e_ready lev_ready lv_done lv_out ea dk de kh_ready kt_done kt_out u_done s_ready "
             "merge_go zero_set zeroed o_done osq ossq orstd eg cleared dve").split()
    m = core.sems("h_", names)
    chunks = lambda t: t[:].rearrange("p (c t) -> p c t", t=P)
    with nc.Block() as block:

        @block.sync
        def _(sp):
            with sp.Fori(1, HH) as i:
                load_head(sp, core, a, i)
            sp.wait_ge(core.wt_free, HH)
            load_q(sp, core, a, 0)
            sp.wait_ge(core.ww_free, HH)
            load_keys(sp, core, a, 0)

        @block.gpsimd
        def _(g):
            for t in (*qe, *ke):
                g.memset(t[:], 0.0).then_inc(m["cleared"], 1)
            g.memset(zero[:], 0.0).then_inc(m["zero_set"], 1)
            g.wait_ge(m["zero_set"], 1)
            g.wait_ge(m["q_ready"], 1)
            with g.Fori(0, (SLOTS + BLK) // BLK) as r:
                g.dma_start(core.pad[bass.ts(r, BLK)], zero[:]).then_inc(m["zeroed"], 16)
            g.wait_ge(m["zeroed"], 16 * ((SLOTS + BLK) // BLK))

        @block.tensor
        def _(pe):
            with pe.Fori(0, HH) as i:
                pe.wait_ge(core.wt_in, i * 32 + 32)
                for j, T, free, ready in ((0, TQ, m["s_ready"], m["q_ready"]), (1, TF, m["o_free"], m["f_ready"])):
                    pe.wait_ge(free, i + 1)
                    for half in range(2):
                        for kt in range(KT):
                            last = nc.tensor.matmul(T[:, half * HALF:(half + 1) * HALF], wt[:, j, kt],
                                                    nT[:, kt, half * HALF:(half + 1) * HALF],
                                                    start=kt == 0, stop=kt == KT - 1)
                    last.then_inc(ready, 1)
                pe.wait_ge(core.ww_in, i * 32 + 32)
                for t in range(NT):
                    if t >= 2:
                        pe.wait_ge(m["tok_out"], i * NT + (t - 1))
                    for kt in range(KT):
                        last = nc.tensor.matmul(TOK[t % 2], nT[:, kt, t * P:(t + 1) * P], ww[:, kt],
                                                start=kt == 0, stop=kt == KT - 1)
                        if t == 0 and kt == 0:
                            last.then_inc(core.wt_free, 1)
                    last.then_inc(m["tok_ready"], 1)
                    pe.wait_ge(m["lev_ready"], i * (LEVELS + 1) + t + 1)
                    qs, ks = (q, kf) if t == 0 else (qe[(t - 1) % 2], ke[(t - 1) % 2])
                    for half in range(2):
                        if t > 0:
                            pe.wait_ge(m["lv_out"], i * 16 + (2 * t - 1 + half))
                        for c in range(half * 4, half * 4 + 4):
                            last = nc.tensor.matmul(LV[half][:, (c % 4) * P:(c % 4 + 1) * P], ks[:, c * P:(c + 1) * P],
                                                    qs[:, c * P:(c + 1) * P], start=True, stop=True)
                        last.then_inc(m["lv_done"], 1)
                    if t == 2:
                        pe.wait_ge(m["kh_ready"], i + 1)
                        for c in range(NT):
                            last = nc.tensor.transpose(U[:, c * P:(c + 1) * P], kh[:, c * P:(c + 1) * P], k.ident[:])
                        last.then_inc(m["kt_done"], 1)
                    if t == 5:
                        pe.wait_ge(m["kt_out"], i + 1)
                        pe.wait_ge(m["tok_out"], i * NT + 5)
                        for c in range(4):
                            last = nc.tensor.matmul(U[:, c * P:(c + 1) * P], kt_sb[:, c], vg[:, c, 0:DK],
                                                    start=True, stop=True)
                pe.wait_ge(m["tok_out"], i * NT + NT)
                for c in range(4, NT - 1):
                    last = nc.tensor.matmul(U[:, c * P:(c + 1) * P], kt_sb[:, c], vg[:, c, 0:DK],
                                            start=True, stop=True)
                    if c == 4:
                        last.then_inc(core.ww_free, 1)
                last.then_inc(m["u_done"], 1)
                pe.wait_ge(m["lv_out"], i * 16 + 16)
                pe.wait_ge(m["s_ready"], i + 2)
                for c in range(NT):
                    last = nc.tensor.matmul(O[:, c * P:(c + 1) * P], at[:, c], vg[:, c, 0:DK],
                                            start=True, stop=c == 0)
                    if c:
                        last = nc.tensor.matmul(O[:, c * P:(c + 1) * P], qh[:, c * P:(c + 1) * P], st[:, c],
                                                start=False, stop=True)
                last.then_inc(m["o_done"], 1)

        @block.scalar
        def _(act):
            def tok(i, t):
                act.wait_ge(m["tok_ready"], i * NT + t + 1)
                nc.scalar.copy(vg[:, t], TOK[t % 2]).then_inc(m["tok_out"], 1)

            with act.Fori(0, HH) as i:
                act.wait_ge(m["q_ready"], i + 1)
                nc.scalar.activation(e2[:], TQ, ACT.Sigmoid).then_inc(m["eq"], 1)
                act.wait_ge(m["f_ready"], i + 1)
                nc.scalar.activation(e1[:], TF, ACT.Sigmoid).then_inc(m["ef"], 1)
                act.preload_act_table_set("natural_log_exp_and_others")
                act.wait_ge(m["fg"], i + 1)
                nc.scalar.activation(lf[:], fg[:], ACT.Ln).then_inc(m["lf"], 1)
                act.wait_ge(m["mix_done"], i + 1)
                tok(i, 0)
                act.wait_ge(m["dk"], i + 1)
                nc.scalar.activation(kh[:], kh[:], ACT.Exp).then_inc(m["de"], 1)
                nc.scalar.activation(qh[:], cum[:], ACT.Exp).then_inc(m["ea"], 1)
                nc.scalar.activation(dec[:], chunks(cum)[:, :, P - 1:P], ACT.Exp).then_inc(m["ea"], 1)
                for l in range(LEVELS):
                    act.wait_ge(m["d_ready"], i * LEVELS + l + 1)
                    nc.scalar.activation(dd[l % 2][:], dd[l % 2][:], ACT.Exp).then_inc(m["e_ready"], 1)
                    tok(i, l + 1)
                    if l == 2:
                        act.wait_ge(m["kt_done"], i + 1)
                        nc.scalar.copy(kt_sb[:], U.rearrange("p (c t) -> p c t", t=P)).then_inc(m["kt_out"], 1)
                act.wait_ge(m["tok_out"], i * NT + NT)
                nc.scalar.activation(gg[:], vg[:, :, DK:2 * DK], ACT.Sigmoid).then_inc(m["eg"], 1)
                act.preload_act_table_set("natural_log_exp_and_others")
                act.wait_ge(m["o_done"], i + 1)
                nc.scalar.activation(og[:], O.rearrange("p (c t) -> p c t", t=P), ACT.Square).then_inc(m["osq"], 1)
                act.wait_ge(m["ossq"], i + 1)
                nc.scalar.activation(ssq[:, 1], ssq[:, 0], ACT.Ln, scale=1.0 / DK, bias=k.eps[:]).then_inc(m["orstd"], 1)
                act.wait_ge(m["orstd"], i * 2 + 1)
                nc.scalar.activation(ssq[:, 1], ssq[:, 1], ACT.Exp, scale=-0.5).then_inc(m["orstd"], 1)

        @block.vector
        def _(dve):
            c = Chain(dve, m["dve"], 25)

            def halves(l, t):
                return t[:].rearrange("p (n two b) -> p n two b", two=2, b=1 << l)

            def distance(i, l):
                B, n = 1 << l, S >> (l + 1)
                s, d = halves(l, cum), halves(l, dd[l % 2])
                r = s[:, :, 0, B - 1:B].to_broadcast([P, n, B])
                if l >= 2:
                    dve.wait_ge(m["lev_ready"], i * (LEVELS + 1) + l)
                c(nc.vector.tensor_tensor(d[:, :, 0], r, s[:, :, 0], ALU.subtract))
                nc.vector.tensor_tensor(d[:, :, 1], s[:, :, 1], r, ALU.subtract).then_inc(m["d_ready"], 1)

            def merge(i, l):
                for half in range(2):
                    dve.wait_ge(m["lv_done"], i * 16 + (2 * l + half + 1))
                    if l:
                        dve.wait_ge(m["lv_out"], i * 16 + (2 * l - 1 + half))
                    dve.sem_inc(m["merge_go"], 1)
                    src = LV[half].rearrange("p (c t) -> p c t", t=P)
                    dst = at[:, half * 4:half * 4 + 4]
                    if l == 0:
                        nc.vector.tensor_tensor(dst, src, k.ident[:].unsqueeze(1).to_broadcast([P, 4, P]),
                                                ALU.mult).then_inc(m["lv_out"], 1)
                    else:
                        nc.vector.copy_predicated(dst, k.lmask[:, l - 1].unsqueeze(1).to_broadcast([P, 4, P]),
                                                  src).then_inc(m["lv_out"], 1)

            dve.sem_inc(m["s_ready"], 1)
            dve.sem_inc(m["o_free"], 1)
            dve.sem_inc(m["mix_done"], 1)
            dve.wait_ge(m["cleared"], 4)
            with dve.Fori(0, HH) as i:
                c.round(i)
                dve.wait_ge(m["eq"], i + 1)
                c(nc.vector.tensor_tensor(q[:], TQ, e2[:], ALU.mult))
                dve.wait_ge(m["ef"], i + 1)
                nc.vector.tensor_scalar(fg[:], e1[:], k.oml[:, bass.ds(i, 1)], k.lb[:, bass.ds(i, 1)], ALU.mult,
                                        ALU.add).then_inc(m["fg"], 1)
                dve.wait_ge(m["fg"], i + 1)
                nc.vector.tensor_scalar(kf[:], fg[:], -1.0, 1.0, ALU.mult, ALU.add).then_inc(m["lev_ready"], 1)
                dve.wait_ge(m["lf"], i + 1)
                c.link(nc.vector.tensor_tensor_scan(cum[:], k.reset[:], lf[:], 0.0, ALU.mult, ALU.add))
                nc.vector.tensor_tensor(chunks(kh), chunks(cum)[:, :, P - 1:P].to_broadcast([P, NT, P]), chunks(cum),
                                        ALU.subtract).then_inc(m["dk"], 1)
                distance(i, 0)
                dve.wait_ge(m["de"], i + 1)
                nc.vector.tensor_tensor(kh[:], kh[:], kf[:], ALU.mult).then_inc(m["kh_ready"], 1)
                dve.wait_ge(m["ea"], i * 2 + 2)
                dve.wait_ge(m["lev_ready"], i * (LEVELS + 1) + 1)
                c(nc.vector.tensor_tensor(qh[:], qh[:], q[:], ALU.mult))
                for l in range(LEVELS):
                    if l + 1 < LEVELS:
                        distance(i, l + 1)
                    dve.wait_ge(m["e_ready"], i * LEVELS + l + 1)
                    e = halves(l, dd[l % 2])
                    c(nc.vector.tensor_tensor(halves(l, qe[l % 2])[:, :, 1], halves(l, q)[:, :, 1], e[:, :, 1],
                                              ALU.mult))
                    nc.vector.tensor_tensor(halves(l, ke[l % 2])[:, :, 0], halves(l, kf)[:, :, 0], e[:, :, 0],
                                            ALU.mult).then_inc(m["lev_ready"], 1)
                    merge(i, l)
                merge(i, LEVELS)
                dve.wait_ge(m["u_done"], i + 1)
                Uc = U.rearrange("p (c t) -> p c t", t=P)
                c.link(nc.vector.tensor_copy(st[:, 1], Uc[:, 0]))
                for ch in range(1, NT - 1):
                    ins = nc.vector.scalar_tensor_tensor(st[:, ch + 1], st[:, ch], dec[:, ch:ch + 1], Uc[:, ch],
                                                         ALU.mult, ALU.add)
                    if ch < NT - 2:
                        c.link(ins)
                ins.then_inc(m["s_ready"], 1)
                dve.wait_ge(m["eg"], i + 1)
                c.link(nc.vector.tensor_tensor(gg[:], gg[:], vg[:, :, DK:2 * DK], ALU.mult))
                c.link(nc.vector.tensor_tensor(gg[:], gg[:], k.g_hg[:].unsqueeze(1).to_broadcast([P, NT, DK]),
                                               ALU.mult))
                dve.wait_ge(m["osq"], i + 1)
                nc.vector.tensor_reduce(ssq[:, 0], og[:], AX.X, ALU.add).then_inc(m["ossq"], 1)
                dve.wait_ge(m["orstd"], i * 2 + 2)
                nc.vector.tensor_tensor(og[:], O.rearrange("p (c t) -> p c t", t=P),
                                        ssq[:, 1].unsqueeze(2).to_broadcast([P, NT, P]), ALU.mult).then_inc(m["o_free"], 1)
                dve.wait_ge(m["o_free"], i + 2)
                nc.vector.tensor_tensor(mixed[:, :, bass.ds(NSA_W + i * DK, DK)], og[:], gg[:],
                                        ALU.mult).then_inc(m["mix_done"], 1)
                c.end()


def load_keys(sp, core, a, g):
    win = a["w_in"][0].rearrange("(t p) n -> p t n", p=P)
    for j, col in enumerate((C_KS, C_KW)):
        sp.dma_start(core.wk[:, :, j * DH:(j + 1) * DH],
                     win[:, :, col + g * DH:col + (g + 1) * DH]).then_inc(core.wk_in, 16)
    for j, col in enumerate((C_KC, C_VC)):
        sp.dma_start(core.wc[:, :, j * DH:(j + 1) * DH],
                     win[:, :, col + g * DH:col + (g + 1) * DH]).then_inc(core.wc_in, 16)


def load_q(sp, core, a, g):
    win = a["w_in"][0].rearrange("(t p) n -> p t n", p=P)
    sp.dma_start(core.wq[:], win[:, :, C_Q + g * REP * DH:C_Q + (g + 1) * REP * DH]).then_inc(core.wq_in, 16)


def attention(nc, core, a):
    k, nT, mixed, ps = core.k, core.nT, core.mixed, core.ps
    w = Map(core, *R_WORK)
    x = Map(core, *R_X)
    w1 = [x("a_wk1", [P, CM, CHID]), x("a_wv1", [P, CM, CHID])]
    wq, wk, wc = core.wq, core.wk, core.wc
    w.at = core.wqkc_end
    NG3 = 3 * REP
    VW = 2 * DH + NG3
    wv = w("a_wv", [P, KT, VW])
    wk2 = w("a_wk2", [P, 2, 2, DH])
    wv2 = w("a_wv2", [P, 2, DH])
    pos = w("a_pos", [P, 2, CM])
    gqs = w("a_gqs", [P, 1])
    qT = w("a_qT", [P, PAIRS, S])
    sq = w("a_sq", [P, S])
    rs = w("a_rs", [P, S])
    ksD = w("a_ksD", [P, S])
    kwD = w("a_kwD", [P, S])
    kcD = w("a_kcD", [P, NC])
    vc = w("a_vc", [NC, DH])
    TS = CSTR // 2
    xc = [w("a_xk", [P, 2, S // 2]), w("a_xv", [P, 2, S // 2])]
    sg = w("a_sg", [P, 2, 2, DH])
    hid = w("a_hid", [P, 2, 2, DH])
    vt = w("a_vt", [P, NT, VW])
    pb = [w("a_p0", [P, 2, S]), w("a_p1", [P, 2, S])]
    pT = w("a_pT", [P, 4, HALF])
    nmx = w("a_nmx", [P, 4, 4])
    sums = w("a_sums", [P, 2, 2, 3])
    coef = w("a_coef", [P, 2, 2, 4])
    inv = w("a_inv", [P, 2, 3])
    wo = w("a_wo", [P, 2, 4, DH])
    oT = w("a_oT", [P, 4 * P])
    T3 = [ps[:, j * 2 * HALF:(j + 1) * 2 * HALF] for j in range(4)]
    SC = ps[:, 0:4 * HALF].rearrange("p (h n) -> p h n", h=2)
    PT = [ps[:, 4 * HALF:5 * HALF], ps[:, 5 * HALF:6 * HALF]]
    OT = ps[:, 6 * HALF:7 * HALF]
    OB = ps[:, 7 * HALF:8 * HALF]
    HID = ps[:, 2 * HALF:2 * HALF + 4 * DH].rearrange("p (v h c) -> p v h c", v=2, h=2)
    KC2 = ps[:, 3 * HALF:3 * HALF + NC]
    VC2 = ps[0:NC, 3 * HALF + DH:3 * HALF + 2 * DH]
    VB = [ps[:, 2 * HALF:2 * HALF + VW], ps[:, 3 * HALF:3 * HALF + VW]]

    units = [(p, i, kind) for p in range(PAIRS) for i in range(NT) for kind in range(2)]
    NU = len(units)
    NV = NU // 2

    def tiles(u):
        _, i, kind = units[u]
        if kind == 0:
            return [(1, j * P, P, j) for j in range(i + 1)]
        first = max(0, i - WINDOW // P)
        out = [(2, (j - first) * P, P, j) for j in range(first, i + 1)]
        return out + [(0, len(out) * P, (CSTR // 2) * i + 7, 0)]

    chunks, of_unit = [], []
    for u in range(NU):
        mine = []
        t = tiles(u)
        for j in range(0, len(t), 2):
            mine.append(len(chunks))
            chunks.append((u, t[j:j + 2]))
        of_unit.append(mine)
    on_act = set()
    for mine in of_unit:
        on_act.update(mine[:(len(mine) + 1) // 2])
    n_act, n_dve, out_at = 0, 0, []
    for n in range(len(chunks)):
        if n in on_act:
            n_act += 1
            out_at.append(("A", n_act))
        else:
            n_dve += 1
            out_at.append(("D", n_dve))

    names = ("w1_in w2_in wv_in w_free pk_done pc_done pq_done sq_ready n_done n_out rs_ready "
             "normed pc_out v_done v_out hid_done sig hid_ready c2_done kc_ready kcopy s_done "
             "m_ready p_ready t_done gq_done ptA ptD o_done o_out ot_out o_turned dve act").split()
    m = core.sems("a_", names)
    win = a["w_in"][0].rearrange("(t p) n -> p t n", p=P)

    def out_wait(eng, g, n):
        which, at = out_at[n]
        if which == "A":
            eng.wait_ge(m["ptA"], g * n_act + at)
        else:
            eng.wait_ge(m["ptD"], g * n_dve + at)

    with nc.Block() as block:

        @block.sync
        def _(sp):
            for g in range(GROUPS):
                if g:
                    sp.wait_ge(m["w_free"], g + 1)
                    load_keys(sp, core, a, g)
                    load_q(sp, core, a, g)
                for j, col in enumerate((C_VS, C_VW)):
                    sp.dma_start(wv[:, :, j * DH:(j + 1) * DH],
                                 win[:, :, col + g * DH:col + (g + 1) * DH]).then_inc(m["wv_in"], 16)
                sp.dma_start(wv[:, :, 2 * DH:VW],
                             win[:, :, C_GATE + g * NG3:C_GATE + (g + 1) * NG3]).then_inc(m["wv_in"], 16)

        @block.tensor
        def _(pe):
            def project(out, cols):
                for half in range(2):
                    for kt in range(KT):
                        last = nc.tensor.matmul(out[:, half * HALF:(half + 1) * HALF], cols(kt),
                                                nT[:, kt, half * HALF:(half + 1) * HALF],
                                                start=kt == 0, stop=kt == KT - 1)
                return last

            def squares(out):
                for half in range(2):
                    last = nc.tensor.matmul(out[:, half * HALF:(half + 1) * HALF], k.halves[:],
                                            sq[:, half * HALF:(half + 1) * HALF], start=True, stop=True)
                last.then_inc(m["n_done"], 1)

            def scores(g, u):
                p, i, kind = units[u]
                if u:
                    pe.wait_ge(m["p_ready"], g * 2 * NU + 2 * u)
                parts = []
                if kind == 0:
                    for c in range(0, (i + 1) * P, HALF):
                        parts.append((ksD, c, c, min(HALF, (i + 1) * P - c)))
                else:
                    first = max(0, i - WINDOW // P)
                    width = (i + 1 - first) * P
                    for c in range(0, width, HALF):
                        parts.append((kwD, first * P + c, c, min(HALF, width - c)))
                    parts.append((kcD, 0, width, (CSTR // 2) * i + 7))
                for src, key, col, n in parts:
                    for h in range(2):
                        r = slice(h * DH, (h + 1) * DH)
                        last = nc.tensor.matmul(SC[:, h, col:col + n], qT[r, p, i * P:(i + 1) * P],
                                                src[r, key:key + n], start=True, stop=True)
                        if u == 0 and key == 0 and h == 0:
                            last.then_inc(m["w_free"], 1)
                last.then_inc(m["s_done"], 1)

            def turn(g, n):
                u, ts = chunks[n]
                if n >= 2:
                    out_wait(pe, g, n - 2)
                pe.wait_ge(m["p_ready"], g * 2 * NU + 2 * u + 2)
                for j, (_, col, keys, _) in enumerate(ts):
                    for h in range(2):
                        at = (j * 2 + h) * P
                        last = nc.tensor.transpose(PT[n % 2][0:keys, at:at + P], pb[u % 2][:, h, col:col + keys],
                                                   k.ident[:])
                last.then_inc(m["t_done"], 1)

            def values(g, n):
                u, ts = chunks[n]
                p, i, kind = units[u]
                v = p * NT + i
                out_wait(pe, g, n)
                if kind == 0 and ts[0][3] == 0 and v:
                    pe.wait_ge(m["ot_out"], g * NV + v)
                first = max(0, i - WINDOW // P)
                for j, (br, _, keys, kt) in enumerate(ts):
                    p_ = pT[0:keys, n % 4, j * 2 * P:(j + 1) * 2 * P]
                    if br == 1:
                        for odd in ((kt % 2,) if i else (0, 1)):
                            last = nc.tensor.matmul(OT[odd * DH:(odd + 1) * DH, 0:2 * P], vt[:, kt, 0:DH], p_,
                                                    start=kt < 2, stop=kt >= i - 1)
                    elif br == 2:
                        last = nc.tensor.matmul(OT[DH:P, 2 * P:4 * P], vt[:, kt, DH:2 * DH], p_,
                                                start=kt == first, stop=kt == i)
                    else:
                        last = nc.tensor.matmul(OT[0:DH, 2 * P:4 * P], vc[0:keys], p_, start=True, stop=True)
                if kind == 1 and n == of_unit[u][-1]:
                    last.then_inc(m["o_done"], 1)

            def turn_outputs(g, v):
                pe.wait_ge(m["ot_out"], g * NV + v + 1)
                pe.wait_ge(m["o_out"], g * NV + v + 1)
                for h in range(2):
                    for j in range(2):
                        last = nc.tensor.transpose(OB[:, (h * 2 + j) * P:(h * 2 + j + 1) * P],
                                                   oT[:, ((1 - j) * 2 + h) * P:((1 - j) * 2 + h + 1) * P], k.ident[:])
                last.then_inc(m["o_turned"], 1)

            pe.sem_inc(m["w_free"], 1)
            with pe.Fori(0, GROUPS) as g:
                pe.wait_ge(core.wk_in, g * 32 + 32)
                project(T3[0], lambda kt: wk[:, kt]).then_inc(m["pk_done"], 1)
                pe.wait_ge(core.wc_in, g * 32 + 32)
                project(T3[1], lambda kt: wc[:, kt]).then_inc(m["pc_done"], 1)
                pe.wait_ge(core.wq_in, g * 16 + 16)
                project(T3[2], lambda kt: wq[:, kt, 0:P]).then_inc(m["pq_done"], 1)
                pe.wait_ge(m["sq_ready"], g * 4 + 1)
                pe.wait_ge(m["o_out"], g * NV + 1)
                squares(T3[3])
                pe.wait_ge(m["wv_in"], g * 48 + 48)
                pe.wait_ge(m["pc_out"], g * 8 + 8)
                for t in range(NT):
                    if t >= 2:
                        pe.wait_ge(m["v_out"], g * NT + (t - 1))
                    for kt in range(KT):
                        last = nc.tensor.matmul(VB[t % 2], nT[:, kt, t * P:(t + 1) * P], wv[:, kt],
                                                start=kt == 0, stop=kt == KT - 1)
                    last.then_inc(m["v_done"], 1)
                pe.wait_ge(m["sq_ready"], g * 4 + 2)
                pe.wait_ge(m["n_out"], g * 4 + 1)
                squares(T3[3])
                pe.wait_ge(m["normed"], g * 4 + 1)
                project(T3[0], lambda kt: wq[:, kt, P:2 * P]).then_inc(m["pq_done"], 1)
                pe.wait_ge(m["v_out"], g * NT + NT)
                pe.wait_ge(m["w1_in"], 64)
                for kv in range(2):
                    for half in range(2):
                        for t in range(CM):
                            last = nc.tensor.matmul(HID[:, kv, half, 0:NC], w1[kv][:, t, half * P:(half + 1) * P],
                                                    xc[kv][:, t // TS, t:t + (NC - 1) * TS + 1:TS],
                                                    start=t == 0, stop=t == CM - 1)
                last.then_inc(m["hid_done"], 1)
                pe.wait_ge(m["sq_ready"], g * 4 + 3)
                pe.wait_ge(m["n_out"], g * 4 + 2)
                squares(T3[3])
                pe.wait_ge(m["hid_ready"], g * 4 + 4)
                pe.wait_ge(m["w2_in"], 48)
                for half in range(2):
                    nc.tensor.matmul(KC2, wk2[:, half].rearrange("p a d -> p (a d)"), hid[:, 0, half, 0:NC],
                                     start=half == 0, stop=half == 1)
                for half in range(2):
                    last = nc.tensor.matmul(VC2, hid[:, 1, half, 0:NC], wv2[:, half], start=half == 0, stop=half == 1)
                last.then_inc(m["c2_done"], 1)
                pe.wait_ge(m["sq_ready"], g * 4 + 4)
                pe.wait_ge(m["n_out"], g * 4 + 3)
                nc.tensor.matmul(T3[3][:, 0:NC], k.halves[:], sq[:, 0:NC], start=True, stop=True).then_inc(m["n_done"], 1)
                pe.wait_ge(m["normed"], g * 4 + 4)
                pe.wait_ge(m["kcopy"], g * 3 + 3)
                for u in range(NU + 2):
                    if u < NU:
                        scores(g, u)
                    mine = of_unit[u - 1] if 0 < u <= NU else []
                    for n in mine[:2]:
                        turn(g, n)
                    if u > 1 and units[u - 2][2] == 1:
                        turn_outputs(g, (u - 2) // 2)
                    for n in mine[2:]:
                        turn(g, n)
                        values(g, n - 2)
                    for n in mine[-2:]:
                        values(g, n)

        @block.scalar
        def _(act):
            for kv, name in enumerate(("cmp_wk1", "cmp_wv1")):
                act.dma_start(w1[kv][:], a[name][0].rearrange("(m p) n -> p m n", p=P)).then_inc(m["w1_in"], 16)
            with nc.allow_non_contiguous_dma(reason="positions, 16 numbers of a partition"):
                for kv, name in enumerate(("cmp_pos_k", "cmp_pos_v")):
                    act.dma_start(pos[:, kv], a[name][0].rearrange("(m l) d -> (l d) m", l=2)).then_inc(m["w1_in"], 16)
            for j in range(2):
                act.dma_start(wk2[:, :, j], a["cmp_wk2"][0].rearrange("(h p) d -> p h d", p=P)).then_inc(m["w2_in"], 16)
            act.dma_start(wv2[:], a["cmp_wv2"][0].rearrange("(h p) d -> p h d", p=P)).then_inc(m["w2_in"], 16)

            def out_of(g, n):
                act.wait_ge(m["t_done"], g * len(chunks) + n + 1)
                nk = chunks[n][1][0][2]
                wd = len(chunks[n][1]) * 2 * P
                nc.scalar.copy(pT[0:nk, n % 4, 0:wd], PT[n % 2][0:nk, 0:wd]).then_inc(m["ptA"], 1)

            def outputs(g, v):
                act.wait_ge(m["o_done"], g * NV + v + 1)
                nc.scalar.copy(oT[:], OT).then_inc(m["ot_out"], 1)

            def inverse_norm(g, j, n):
                act.wait_ge(m["n_done"], g * 4 + j + 1)
                if j:
                    act.wait_ge(m["normed"], g * 4 + j)
                nc.scalar.activation(rs[:, 0:n], T3[3][:, 0:n], ACT.Ln, bias=k.eps[:]).then_inc(m["n_out"], 1)
                act.wait_ge(m["n_out"], g * 4 + j + 1)
                nc.scalar.activation(rs[:, 0:n], rs[:, 0:n], ACT.Exp, scale=-0.5).then_inc(m["rs_ready"], 1)

            def v_evac(g, t):
                act.wait_ge(m["v_done"], g * NT + t + 1)
                nc.scalar.copy(vt[:, t], VB[t % 2]).then_inc(m["v_out"], 1)

            with act.Fori(0, GROUPS) as g:
                act.wait_ge(m["pk_done"], g + 1)
                nc.scalar.activation(sq[:], T3[0], ACT.Square).then_inc(m["sq_ready"], 1)
                act.wait_ge(m["pq_done"], g * 2 + 1)
                inverse_norm(g, 0, S)
                nc.scalar.activation(sq[:], T3[2], ACT.Square).then_inc(m["sq_ready"], 1)
                for t in range(NT):
                    v_evac(g, t)
                inverse_norm(g, 1, S)
                act.wait_ge(m["pq_done"], g * 2 + 2)
                nc.scalar.activation(sq[:], T3[0], ACT.Square).then_inc(m["sq_ready"], 1)
                act.wait_ge(m["v_out"], g * NT + NT)
                nc.scalar.activation(vt[:, :, 2 * DH:VW], vt[:, :, 2 * DH:VW], ACT.Sigmoid).then_inc(m["sig"], 1)
                act.wait_ge(m["hid_done"], g + 1)
                for kv in range(2):
                    for half in range(2):
                        nc.scalar.activation(sg[:, kv, half, 0:NC], HID[:, kv, half, 0:NC], ACT.Sigmoid).then_inc(m["sig"], 1)
                act.preload_act_table_set("natural_log_exp_and_others")
                inverse_norm(g, 2, S)
                act.wait_ge(m["c2_done"], g + 1)
                nc.scalar.activation(sq[:, 0:NC], KC2, ACT.Square).then_inc(m["sq_ready"], 1)
                inverse_norm(g, 3, NC)
                for u in range(NU + 2):
                    mine = [n for n in of_unit[u - 1] if n in on_act] if 0 < u <= NU else []
                    if u > 1 and units[u - 2][2] == 1:
                        outputs(g, (u - 2) // 2)
                    if mine:
                        out_of(g, mine.pop(0))
                    if u < NU:
                        p, i, kind = units[u]
                        v = p * NT + i
                        for h in range(2):
                            act.wait_ge(m["m_ready"], g * 2 * NU + 2 * u + h + 1)
                            if kind == 0:
                                parts = [(1, 0, (i + 1) * P)]
                            else:
                                width = min(i + 1, WINDOW // P + 1) * P
                                parts = [(2, 0, width), (0, width, (CSTR // 2) * i + 7)]
                            for br, col, n in parts:
                                ins = nc.scalar.activation(pb[u % 2][:, h, col:col + n], SC[:, h, col:col + n],
                                                           ACT.Exp, bias=nmx[:, (u % 2) * 2 + br // 2, h:h + 1],
                                                           accum_out=sums[:, v % 2, h, br:br + 1])
                            ins.then_inc(m["p_ready"], 1)
                            if mine:
                                out_of(g, mine.pop(0))
                    for n in mine:
                        out_of(g, n)

        @block.vector
        def _(dve):
            c = Chain(dve, m["dve"], 141)

            def out_of(g, n):
                dve.wait_ge(m["t_done"], g * len(chunks) + n + 1)
                nk = chunks[n][1][0][2]
                wd = len(chunks[n][1]) * 2 * P
                nc.vector.tensor_copy(pT[0:nk, n % 4, 0:wd], PT[n % 2][0:nk, 0:wd]).then_inc(m["ptD"], 1)

            def mask_and_max(g, u):
                p, i, kind = units[u]
                dve.wait_ge(m["s_done"], g * NU + u + 1)
                two = lambda ap, n: ap.unsqueeze(1).to_broadcast([P, 2, n])
                if kind == 0:
                    d = SC[:, :, i * P:(i + 1) * P]
                    c.link(nc.vector.tensor_tensor(d, d, two(k.causal[:], P), ALU.add))
                    for h in range(2):
                        nc.vector.tensor_reduce(nmx[:, 0, h:h + 1], SC[:, h, 0:(i + 1) * P], AX.X, ALU.max,
                                                negate=True).then_inc(m["m_ready"], 1)
                    return
                width, n = min(i + 1, WINDOW // P + 1) * P, (CSTR // 2) * i + 7
                d = SC[:, :, width - P:width]
                c(nc.vector.tensor_tensor(d, d, two(k.causal[:], P), ALU.add))
                if i >= WINDOW // P:
                    d = SC[:, :, 0:P]
                    c(nc.vector.tensor_tensor(d, d, two(k.far[:], P), ALU.add))
                d = SC[:, :, width:width + n]
                c.link(nc.vector.tensor_tensor(d, d, two(k.cneg[:, i, 0:n], n), ALU.add))
                c(nc.vector.tensor_reduce(nmx[:, 2, 0:2], d, AX.X, ALU.max, negate=True))
                for h in range(2):
                    nc.vector.tensor_reduce(nmx[:, 3, h:h + 1], SC[:, h, 0:width], AX.X, ALU.max,
                                            negate=True).then_inc(m["m_ready"], 1)

            def combine(g, v):
                p, i = v // NT, v % NT
                dve.wait_ge(m["o_turned"], g * NV + v + 1)
                cf = coef[:, v % 2]
                c.link(nc.vector.reciprocal(inv[:], sums[:, v % 2]))
                gates = vt[:, i, 2 * DH + p * 6:2 * DH + p * 6 + 6].rearrange("p (h b) -> p h b", h=2)
                c(nc.vector.tensor_tensor(cf[:, :, 0:2], inv[:, :, 0:3:2], gates[:, :, 0:3:2], ALU.mult))
                both = lambda ap: ap[:, :, 1:2].to_broadcast([P, 2, 2])
                c.link(nc.vector.tensor_tensor(cf[:, :, 2:4], both(inv), both(gates), ALU.mult))
                if i == 0:
                    c(nc.vector.memset(cf[:, :, 3:4], 0.0))
                    c.link(nc.vector.tensor_scalar(cf[:, :, 0:1], cf[:, :, 0:1], k.cmask[:, 0, 0:1], None, ALU.mult))
                flat = wo[:].rearrange("p h b d -> p (h b) d")
                nc.vector.tensor_tensor(flat, OB.rearrange("p (x d) -> p x d", d=DH),
                                        cf.rearrange("p h b -> p (h b)").unsqueeze(2).to_broadcast([P, 8, DH]),
                                        ALU.mult).then_inc(m["o_out"], 1)
                dve.wait_ge(m["o_out"], g * NV + v + 2)
                c.link(nc.vector.tensor_reduce(
                    mixed[:, i, bass.ds(g * REP * DH + p * P, P)].rearrange("p (h d) -> p h d", h=2),
                    wo[:].rearrange("p h b d -> p h d b"), AX.X, ALU.add))

            dve.sem_inc(m["o_out"], 1)
            nc.vector.tensor_scalar(gqs[:], k.gq[:], float(DH) ** -0.5, None, ALU.mult).then_inc(m["gq_done"], 1)
            with dve.Fori(0, GROUPS) as g:
                c.round(g)
                dve.wait_ge(m["pc_done"], g + 1)
                dve.wait_ge(m["w1_in"], 64)
                for kv in range(2):
                    src = T3[1][kv * DH:(kv + 1) * DH].rearrange("p (n two) -> p two n", two=2)
                    for par in range(2):
                        r = slice(par * DH, (par + 1) * DH)
                        for first in range(2):
                            at = pos[r, kv, first * TS:(first + 1) * TS].unsqueeze(1).to_broadcast([DH, S // CSTR, TS])
                            nc.vector.tensor_tensor(xc[kv][r, first].rearrange("p (c t) -> p c t", t=TS),
                                                    src[:, par].rearrange("p (c t) -> p c t", t=TS), at,
                                                    ALU.add).then_inc(m["pc_out"], 1)
                dve.wait_ge(m["rs_ready"], g * 4 + 1)
                lo, hi = slice(0, DH), slice(DH, P)
                c(nc.vector.scalar_tensor_tensor(ksD[lo], T3[0][lo], k.gkk[lo], rs[lo], ALU.mult, ALU.mult))
                nc.vector.scalar_tensor_tensor(kwD[hi], T3[0][hi], k.gkk[hi], rs[hi], ALU.mult,
                                               ALU.mult).then_inc(m["normed"], 1)
                dve.wait_ge(m["normed"], g * 4 + 1)
                nc.vector.tensor_copy(ksD[hi], ksD[lo]).then_inc(m["kcopy"], 1)
                nc.vector.tensor_copy(kwD[lo], kwD[hi]).then_inc(m["kcopy"], 1)
                for j, (src, p) in enumerate(((T3[2], 0), (T3[0], 1))):
                    dve.wait_ge(m["rs_ready"], g * 4 + 2 + j)
                    nc.vector.scalar_tensor_tensor(qT[:, p], src, gqs[:], rs[:], ALU.mult, ALU.mult).then_inc(m["normed"], 1)
                    if j == 0:
                        dve.wait_ge(m["sig"], g * 5 + 5)
                        for kv in range(2):
                            for half in range(2):
                                nc.vector.tensor_tensor(hid[:, kv, half, 0:NC], HID[:, kv, half, 0:NC],
                                                        sg[:, kv, half, 0:NC], ALU.mult).then_inc(m["hid_ready"], 1)
                dve.wait_ge(m["rs_ready"], g * 4 + 4)
                nc.vector.tensor_copy(vc[:], VC2).then_inc(m["kcopy"], 1)
                nc.vector.scalar_tensor_tensor(kcD[:], KC2, k.gkc[:], rs[:, 0:NC], ALU.mult,
                                               ALU.mult).then_inc(m["normed"], 1)
                for u in range(NU + 2):
                    if u < NU:
                        mask_and_max(g, u)
                    if 0 < u <= NU:
                        for n in of_unit[u - 1]:
                            if n not in on_act:
                                out_of(g, n)
                    if u > 1 and units[u - 2][2] == 1:
                        combine(g, (u - 2) // 2)
                c.end()


R_WOUT = (112 * KB, 144 * KB)
R_WU = (144 * KB, 80 * KB, 48 * KB)
R_WD = (176 * KB, 112 * KB, 128 * KB)
NW = 3
R_BLOCK = (1 * KB, 16 * KB)
R_ROUTE = (195 * KB, 196 * KB)
R_TOP = (192 * KB, 207 * KB)


def load_expert(nc, sp, core, a, i, q):
    wu, wd = core.wu[q], core.wd[q]
    e = i * NW + q
    sp.wait_ge(core.wu_free[q], i + 1)
    for j, name in enumerate(("moe_w1", "moe_w3")):
        sp.dma_start(wu[:, j], a[name][0, bass.ds(e, 1)].rearrange("o (p k) f -> p (o k) f", p=P)).then_inc(core.wu_in[q], 16)
    sp.wait_ge(core.wd_free[q], i + 1)
    sp.dma_start(wd[:], a["moe_w2"][0, bass.ds(e, 1)].rearrange("o (j p) d -> p (o j) d", p=P)).then_inc(core.wd_in[q], 16)


def out_projection(nc, core, a):
    k, ps = core.k, core.ps
    mixed, mT = core.mixed, core.nT
    h = core.h = core.sb("o_h", [P, NT, D], R_X[0])
    n2 = core.n2 = core.mixed
    wout = core.sb("o_wout", [P, KT, D], R_WOUT[0])
    t_ = Map(core, *R_TOP)
    lg = core.lg = t_("o_lg", [P, NT, NG + NE])
    ss = t_("o_ss", [P, NT])
    hs = t_("o_hs", [P, NT])
    gf = t_("o_gf", [P, D])
    nT2 = t_("o_nT", [P, KT, P])
    sq = t_("o_sq", [P, D])
    names = ("wout_in gf_in x_in sum rstd scaled mt_done mtA mtD pr_done added hsum hr n2_ready t_done t_out "
             "lg_done lg_out act").split()
    m = core.sems("o_", names)
    mt_ring = [ps[:, b * HALF:(b + 1) * HALF] for b in range(4)]
    H = [ps[:, 4 * HALF:6 * HALF], ps[:, 6 * HALF:8 * HALF]]
    NTB = ps[:, 0:2 * HALF]
    LG = ps[:, 2 * HALF:2 * HALF + NG + NE]
    HT = NT // 2
    with nc.Block() as block:

        @block.sync
        def _(sp):
            sp.dma_start(wout[:], a["w_out"][0].rearrange("(t p) n -> p t n", p=P)).then_inc(m["wout_in"], 16)
            sp.dma_start(h[:], a["x"][0].rearrange("(t p) d -> p t d", p=P)).then_inc(m["x_in"], 16)
            sp.dma_start(gf[:], a["ffn_norm_g"][0].partition_broadcast(P)).then_inc(m["gf_in"], 16)
            load_expert(nc, sp, core, a, 0, 0)

        @block.tensor
        def _(pe):
            for q in range(NW):
                pe.sem_inc(core.wu_free[q], 1)
                pe.sem_inc(core.wd_free[q], 1)

            def turn_mixed(half):
                pe.wait_ge(m["scaled"], (half + 1) * HT)
                for kt in range(KT):
                    n = half * KT + kt
                    if n >= 4:
                        pe.wait_ge((m["mtA"], m["mtD"])[n % 2], (n - 4) // 2 + 1)
                    for j in range(HT):
                        last = nc.tensor.transpose(mt_ring[n % 4][:, j * P:(j + 1) * P],
                                                   mixed[:, half * HT + j, kt * P:(kt + 1) * P], k.ident[:])
                    last.then_inc(m["mt_done"], 1)

            def turn_n2(t):
                pe.wait_ge(m["n2_ready"], t + 1)
                if t == 0:
                    pe.wait_ge(m["mtA"], KT)
                    pe.wait_ge(m["mtD"], KT)
                else:
                    pe.wait_ge(m["t_out"], t)
                for kt in range(KT):
                    last = nc.tensor.transpose(NTB[:, kt * P:(kt + 1) * P], n2[:, t, kt * P:(kt + 1) * P], k.ident[:])
                last.then_inc(m["t_done"], 1)

            def logits(t):
                pe.wait_ge(m["t_out"], t + 1)
                if t:
                    pe.wait_ge(m["lg_out"], t)
                for kt in range(KT):
                    last = nc.tensor.matmul(LG, nT2[:, kt], k.wr[:, kt], start=kt == 0, stop=kt == KT - 1)
                last.then_inc(m["lg_done"], 1)

            def project(t):
                if t >= 2:
                    pe.wait_ge(m["added"], t - 1)
                for half in range(2):
                    for kt in range(KT):
                        last = nc.tensor.matmul(H[t % 2][:, half * HALF:(half + 1) * HALF], mT[:, kt, t * P:(t + 1) * P],
                                                wout[:, kt, half * HALF:(half + 1) * HALF],
                                                start=kt == 0, stop=kt == KT - 1)
                last.then_inc(m["pr_done"], 1)

            turn_mixed(0)
            pe.wait_ge(m["mtA"], KT // 2)
            pe.wait_ge(m["mtD"], KT // 2)
            pe.wait_ge(m["wout_in"], 16)
            project(0)
            turn_mixed(1)
            project(1)
            turn_n2(0)
            for t in range(2, NT):
                if t == HT:
                    pe.wait_ge(m["mtA"], KT)
                    pe.wait_ge(m["mtD"], KT)
                project(t)
                logits(t - 2)
                turn_n2(t - 1)
            logits(NT - 2)
            turn_n2(NT - 1)
            logits(NT - 1)

        @block.scalar
        def _(act):
            c = Chain(act, m["act"])
            for half in range(2):
                for t in range(half * HT, half * HT + HT):
                    c.link(nc.scalar.activation(sq[:, 0:NSA_W], mixed[:, t, 0:NSA_W], ACT.Square,
                                                accum_out=ss[:, t:t + 1]))
                s = ss[:, half * HT:(half + 1) * HT]
                c.link(nc.scalar.activation(s, s, ACT.Ln, scale=1.0 / NSA_W, bias=k.eps[:]))
                nc.scalar.activation(s, s, ACT.Exp, scale=-0.5).then_inc(m["rstd"], 1)

            def mixed_out(half):
                for kt in range(0, KT, 2):
                    n = half * KT + kt
                    act.wait_ge(m["mt_done"], n + 1)
                    dst = mT[:, kt, half * HALF:(half + 1) * HALF]
                    if kt < NSA_W // P:
                        ins = nc.scalar.mul(dst, mt_ring[n % 4], k.g_nsa[:, kt:kt + 1])
                    else:
                        ins = nc.scalar.copy(dst, mt_ring[n % 4])
                    ins.then_inc(m["mtA"], 1)

            def n2_out(t):
                act.wait_ge(m["t_done"], t + 1)
                if t:
                    act.wait_ge(m["lg_done"], t)
                nc.scalar.copy(nT2[:].rearrange("p k t -> p (k t)"), NTB).then_inc(m["t_out"], 1)

            mixed_out(0)
            mixed_out(1)
            for t in range(NT):
                act.wait_ge(m["added"], t + 1)
                c.link(nc.scalar.activation(sq[:], h[:, t], ACT.Square, accum_out=hs[:, t:t + 1]))
                c.link(nc.scalar.activation(hs[:, t:t + 1], hs[:, t:t + 1], ACT.Ln, scale=1.0 / D, bias=k.eps[:]))
                nc.scalar.activation(hs[:, t:t + 1], hs[:, t:t + 1], ACT.Exp, scale=-0.5).then_inc(m["hr"], 1)
                if t:
                    n2_out(t - 1)
            n2_out(NT - 1)

        @block.vector
        def _(dve):
            for t in range(NT):
                dve.wait_ge(m["rstd"], t // HT + 1)
                nc.vector.tensor_scalar(mixed[:, t, 0:NSA_W], mixed[:, t, 0:NSA_W], ss[:, t:t + 1], None,
                                        ALU.mult).then_inc(m["scaled"], 1)
            for half in range(2):
                for kt in range(1, KT, 2):
                    n = half * KT + kt
                    dve.wait_ge(m["mt_done"], n + 1)
                    dst = mT[:, kt, half * HALF:(half + 1) * HALF]
                    if kt < NSA_W // P:
                        ins = nc.vector.tensor_scalar(dst, mt_ring[n % 4], k.g_nsa[:, kt:kt + 1], None, ALU.mult)
                    else:
                        ins = nc.vector.tensor_copy(dst, mt_ring[n % 4])
                    ins.then_inc(m["mtD"], 1)
                if half == 0:
                    dve.wait_ge(m["x_in"], 16)
                    dve.wait_ge(m["gf_in"], 16)

            def scale(t):
                dve.wait_ge(m["hr"], t + 1)
                nc.vector.scalar_tensor_tensor(n2[:, t], h[:, t], hs[:, t:t + 1], gf[:], ALU.mult,
                                               ALU.mult).then_inc(m["n2_ready"], 1)

            def take_logits(t):
                dve.wait_ge(m["lg_done"], t + 1)
                nc.vector.tensor_tensor(lg[:, t], LG, k.brt[:], ALU.add).then_inc(m["lg_out"], 1)

            for t in range(NT):
                dve.wait_ge(m["pr_done"], t + 1)
                if t == HT - 1:
                    dve.wait_ge(m["mt_done"], 2 * KT)
                nc.vector.tensor_tensor(h[:, t], h[:, t], H[t % 2], ALU.add).then_inc(m["added"], 1)
                scale(t)
                if t >= 2:
                    take_logits(t - 2)
            take_logits(NT - 2)
            take_logits(NT - 1)


def routing(nc, core, a):
    k, ps, lg = core.k, core.ps, core.lg
    keep = Map(core, *R_ROUTE)
    wt = core.wtok = keep("r_wt", [P, 2, NT])
    slot = core.slot = keep("r_slot", [P, 2, NT], U32)
    nblk = core.nblk = keep("r_nblk", [P, NE], I32)
    first = core.first = keep("r_first", [P, NE + 1], I32)
    w = Map(core, 196 * KB, 207 * KB + 512)
    EXP = [P, NT, NE]
    gd = w("r_gd", [P, NT, NG])
    ge = w("r_ge", [P, NT, NG])
    go = w("r_go", [P, NT, NG])
    s1 = w("r_s1", [P, NT])
    m12 = w("r_m", [P, 2, NT])
    le = w("r_le", EXP)
    ch = [w("r_c0", EXP), w("r_c1", EXP)]
    cand = w("r_cand", EXP)
    both = w("r_both", EXP)
    off = w("r_off", [P, NT + 1, NE])
    cnt = w("r_cnt", [P, 4, NE])
    ci = w("r_ci", [P, NE], I32)
    RANK = ps[:, 0:NT * NE]
    TOT = ps[:, HALF:HALF + NT * NE]
    m = core.sems("r_", "gexp texp picked ranked slots scattered dve gd_ready t_ready".split())
    with nc.Block() as block:

        @block.sync
        def _(sp):
            load_expert(nc, sp, core, a, 0, 1)

        @block.scalar
        def _(act):
            act.wait_ge(m["gd_ready"], 1)
            nc.scalar.activation(ge[:], gd[:], ACT.Exp).then_inc(m["gexp"], 1)
            act.wait_ge(m["t_ready"], 1)
            nc.scalar.activation(wt[:, 1], wt[:, 1], ACT.Exp).then_inc(m["texp"], 1)

        @block.tensor
        def _(pe):
            pe.wait_ge(m["picked"], 1)
            flat = both[:].rearrange("p t e -> p (t e)")
            nc.tensor.matmul(RANK, k.before[:], flat, start=True, stop=True)
            nc.tensor.matmul(TOT, k.ones[:], flat, start=True, stop=True).then_inc(m["ranked"], 1)

        @block.vector
        def _(dve):
            c = Chain(dve, m["dve"])
            v = nc.vector

            def first_of(out, x, top, order, n):
                wide = lambda ap: ap.unsqueeze(2).to_broadcast([P, NT, n])
                c.link(v.tensor_tensor(out[:], x[:], wide(top), ALU.is_equal))
                c.link(v.tensor_tensor(out[:], out[:], order.unsqueeze(1).to_broadcast([P, NT, n]), ALU.mult))
                c.link(v.tensor_reduce(s1[:], out[:], AX.X, ALU.max))
                c.link(v.tensor_tensor(out[:], out[:], wide(s1[:]), ALU.is_equal))

            gl = lg[:, :, 0:NG]
            c.link(v.tensor_reduce(m12[:, 0], gl, AX.X, ALU.max))
            v.tensor_tensor(gd[:], gl, m12[:, 0].unsqueeze(2).to_broadcast([P, NT, NG]),
                            ALU.subtract).then_inc(m["gd_ready"], 1)
            first_of(go, gl, m12[:, 0], k.order[:, NE - NG:NE], NG)
            le4 = le[:].rearrange("p t (g e) -> p t g e", g=NG)
            wide = lambda ap: ap.unsqueeze(3).to_broadcast([P, NT, NG, EPG])
            c.link(v.tensor_tensor(le4, lg[:, :, NG:NG + NE].rearrange("p t (g e) -> p t g e", g=NG), wide(go[:]), ALU.mult))
            c.link(v.tensor_scalar(go[:], go[:], 1.0, -NEG, ALU.subtract, ALU.mult))
            c.link(v.tensor_tensor(le4, le4, wide(go[:]), ALU.add))
            for j in range(2):
                c.link(v.tensor_reduce(m12[:, j], le[:], AX.X, ALU.max))
                first_of(ch[j], le, m12[:, j], k.order[:], NE)
                if j == 0:
                    c.link(v.scalar_tensor_tensor(le[:], ch[0][:], 2 * NEG, le[:], ALU.mult, ALU.add))
            v.tensor_tensor(both[:], ch[0][:], ch[1][:], ALU.add).then_inc(m["picked"], 1)
            v.tensor_tensor(wt[:, 1], m12[:, 1], m12[:, 0], ALU.subtract).then_inc(m["t_ready"], 1)
            dve.wait_ge(m["gexp"], 1)
            c.link(v.tensor_reduce(s1[:], ge[:], AX.X, ALU.add))
            dve.wait_ge(m["texp"], 1)
            c.link(v.tensor_scalar(wt[:, 0], wt[:, 1], 1.0, None, ALU.add))
            c.link(v.tensor_tensor(s1[:], s1[:], wt[:, 0], ALU.mult))
            c.link(v.reciprocal(wt[:, 0], s1[:]))
            c.link(v.tensor_tensor(wt[:, 1], wt[:, 1], wt[:, 0], ALU.mult))
            dve.wait_ge(m["ranked"], 1)
            c.link(v.memset(off[:, 0], 0.0))
            tot = TOT.rearrange("p (t e) -> p t e", e=NE)
            for t in range(NT):
                c.link(v.tensor_tensor(off[:, t + 1], off[:, t], tot[:, t], ALU.add))
            c.link(v.tensor_scalar(ci[:], off[:, NT], float(BLK - 1), None, ALU.add))
            c.link(v.tensor_scalar(ci[:], ci[:], BLK.bit_length() - 1, None, ALU.arith_shift_right))
            c.link(v.tensor_scalar(cnt[:, 0], ci[:], 1.0, None, ALU.max))
            c(v.tensor_copy(nblk[:], cnt[:, 0]))
            c.link(v.memset(cnt[:, 3], 1.0))
            c.link(v.tensor_tensor_scan(cnt[:, 1], cnt[:, 3], cnt[:, 0], 0.0, ALU.mult, ALU.add))
            c.link(v.tensor_tensor(cnt[:, 2], cnt[:, 1], cnt[:, 0], ALU.subtract))
            c(v.tensor_copy(first[:, 1:NE + 1], cnt[:, 1]))
            c.link(v.tensor_copy(first[:, 0:1], cnt[:, 2, 0:1]))
            c.link(v.tensor_scalar(cnt[:, 2], cnt[:, 2], float(BLK), None, ALU.mult))
            c.link(v.tensor_tensor(cand[:], RANK.rearrange("p (t e) -> p t e", e=NE), off[:, 0:NT], ALU.add))
            c.link(v.tensor_tensor(cand[:], cand[:], cnt[:, 2].unsqueeze(1).to_broadcast([P, NT, NE]), ALU.add))
            for j in range(2):
                c.link(v.tensor_tensor(ch[j][:], ch[j][:], cand[:], ALU.mult))
                c.link(v.tensor_reduce(m12[:, j], ch[j][:], AX.X, ALU.add))
                v.tensor_copy(slot[:, j], m12[:, j]).then_inc(m["slots"], 1)

        @block.gpsimd
        def _(g):
            for j in range(2):
                g.wait_ge(m["slots"], j + 1)
                for t in range(NT):
                    g.indirect_dma_start(out=core.pad, out_offset=bass.IndirectOffsetOnAxis(ap=slot[:, j, t:t + 1], axis=0),
                                         in_=core.n2[:, t], in_offset=None).then_inc(m["scattered"], 16)
            g.wait_ge(m["scattered"], 16 * 2 * NT)


def experts(nc, core, a):
    k, ps = core.k, core.ps
    w = Map(core, *R_BLOCK)
    xb = w("m_xb", [BLK, D])
    xT = w("m_xT", [P, KT, BLK])
    sil = w("m_sil", [P, FF])
    hb = w("m_h", [P, FF])
    hT = w("m_hT", [P, FT, BLK])
    yb = w("m_y", [P, HALF])
    XT = ps[:, 0:HALF]
    GATE = ps[0:BLK, HALF:2 * HALF]
    UP = ps[BLK:P, HALF:2 * HALF]
    HTB = ps[:, 2 * HALF:2 * HALF + FT * BLK]
    Y = ps[:, 3 * HALF:4 * HALF]
    m = core.sems("m_", "x_in xt_done xt_out turn_go u_done silu h_ready ht_done ht_out y_done y_out y_st".split())
    ROUNDS = NE // NW
    nb_of = lambda eng: eng.value_load(core.first[0:1, NE:NE + 1], min_val=NE, max_val=MAXBLK)
    with nc.Block() as block:

        @block.sync
        def _(sp):
            sp.wait_ge(m["x_in"], 16)
            load_expert(nc, sp, core, a, 0, 2)
            with sp.Fori(1, ROUNDS) as i:
                for q in range(NW):
                    load_expert(nc, sp, core, a, i, q)
            for q in range(NE % NW):
                load_expert(nc, sp, core, a, ROUNDS, q)

        @block.gpsimd
        def _(g):
            nb = nb_of(g)
            g.dma_start(xb[:], core.pad[0:BLK]).then_inc(m["x_in"], 16)
            with g.Fori(1, nb + 1) as b:
                g.wait_ge(m["xt_done"], b)
                g.dma_start(xb[:], core.pad[bass.ds(b * BLK, BLK)]).then_inc(m["x_in"], 16)

        @block.tensor
        def _(pe):
            def up(b, q, note=None):
                pe.wait_ge(m["xt_out"], b + 1)
                for kt in range(KT):
                    for j, out in enumerate((GATE, UP)):
                        last = nc.tensor.matmul(out, xT[:, kt], core.wu[q][:, j, kt], start=kt == 0, stop=kt == KT - 1)
                        if note is not None and kt == 0 and j == 0:
                            last.then_inc(note, 1)
                last.then_inc(m["u_done"], 1)

            def turn_rows(b):
                pe.wait_ge(m["x_in"], b * 16 + 16)
                pe.sem_inc(m["turn_go"], 1)
                rows = xb[:].rearrange("t (p k) -> t k p", k=KT)
                for kt in range(KT):
                    last = nc.tensor.transpose(XT[:, kt * BLK:(kt + 1) * BLK], rows[:, kt], k.ident[0:BLK, 0:BLK])
                last.then_inc(m["xt_done"], 1)

            def down(b, q):
                pe.wait_ge(m["ht_out"], b + 1)
                pe.wait_ge(m["y_out"], b + 1)
                for j in range(FT):
                    for half in range(2):
                        last = nc.tensor.matmul(Y[half * BLK:(half + 1) * BLK], hT[:, j],
                                                core.wd[q][:, j, half * HALF:(half + 1) * HALF],
                                                start=j == 0, stop=j == FT - 1)
                last.then_inc(m["y_done"], 1)

            def turn_hidden(b, note=None):
                pe.wait_ge(m["h_ready"], b + 1)
                pe.sem_inc(m["turn_go"], 1)
                for j in range(FT):
                    last = nc.tensor.transpose(HTB[:, j * BLK:(j + 1) * BLK], hb[BLK:P, j * P:(j + 1) * P],
                                               k.ident[BLK:P, BLK:P])
                    if note is not None and j == 0:
                        last.then_inc(note, 1)
                last.then_inc(m["ht_done"], 1)

            def step(b, q_up, q_down, boundary):
                up(b, q_up, core.wu_free[q_down] if boundary else None)
                turn_rows(b + 1)
                down(b - 1, q_down)
                turn_hidden(b, core.wd_free[q_down] if boundary else None)

            def rest_of(e, q):
                n = pe.value_load(core.nblk[0:1, bass.ds(e, 1)], min_val=1, max_val=S // BLK)
                at = pe.value_load(core.first[0:1, bass.ds(e, 1)], min_val=0, max_val=MAXBLK)
                with pe.If(n > 1):
                    with pe.Fori(at + 1, at + n) as b:
                        step(b, q, q, False)
                return pe.value_load(core.first[0:1, bass.ds(e + 1, 1)], min_val=1, max_val=MAXBLK)

            turn_rows(0)
            pe.wait_ge(core.wu_in[0], 32)
            up(0, 0)
            turn_rows(1)
            turn_hidden(0)
            def one(i, q):
                nq = (q + 1) % NW
                pe.wait_ge(core.wd_in[q], i * 16 + 16)
                nxt = rest_of(i * NW + q, q)
                pe.wait_ge(core.wu_in[nq], i * 32 + (32 if nq else 64))
                step(nxt, nq, q, True)

            with pe.Fori(0, ROUNDS) as i:
                for q in range(NW):
                    one(i, q)
            one(ROUNDS, 0)
            pe.wait_ge(core.wd_in[1], ROUNDS * 16 + 16)
            nb = rest_of(NE - 1, 1)
            down(nb - 1, 1)

        @block.scalar
        def _(act):
            def silu(b):
                act.wait_ge(m["u_done"], b + 1)
                nc.scalar.activation(sil[BLK:P], GATE, ACT.Silu).then_inc(m["silu"], 1)

            def take(b):
                act.wait_ge(m["y_done"], b + 1)
                act.wait_ge(m["y_st"], b * 32 + 32)
                nc.scalar.copy(yb[:], Y).then_inc(m["y_out"], 1)
                act.wait_ge(m["y_out"], b + 2)
                for half in range(2):
                    act.dma_start(core.pad[bass.ds(b * BLK, BLK), half * HALF:(half + 1) * HALF],
                                  yb[half * BLK:(half + 1) * BLK]).then_inc(m["y_st"], 16)

            act.sem_inc(m["y_out"], 1)
            act.sem_inc(m["y_st"], 32)
            nb = nb_of(act)
            silu(0)
            with act.Fori(1, nb) as b:
                silu(b)
                take(b - 1)
            take(nb - 1)

        @block.vector
        def _(dve):
            def take_rows(b):
                dve.wait_ge(m["xt_done"], b + 1)
                nc.vector.tensor_copy(xT[:].rearrange("p k t -> p (k t)"), XT).then_inc(m["xt_out"], 1)

            nb = nb_of(dve)
            take_rows(0)
            with dve.Fori(0, nb) as b:
                take_rows(b + 1)
                dve.wait_ge(m["silu"], b + 1)
                nc.vector.tensor_tensor(hb[BLK:P], sil[BLK:P], UP, ALU.mult).then_inc(m["h_ready"], 1)
                dve.wait_ge(m["ht_done"], b + 1)
                nc.vector.tensor_copy(hT[:].rearrange("p j t -> p (j t)"), HTB).then_inc(m["ht_out"], 1)
    core.m_y_st, core.nb_of = m["y_st"], nb_of


def combine(nc, core, a, out):
    h, wt, slot = core.h, core.wtok, core.slot
    RING = 4
    y = core.sb("c_y", [P, RING, 2, D], R_MIX[0])
    got = [core.sem(f"c_got{r}") for r in range(RING)]
    part, done, stored = core.sem("c_part"), core.sem("c_done"), core.sem("c_stored")
    go = core.sem("c_go")
    with nc.Block() as block:

        @block.gpsimd
        def _(g):
            nb = core.nb_of(g)
            g.wait_ge(core.m_y_st, nb * 32 + 32)
            g.sem_inc(go, 1)
            for t in range(NT):
                if t >= RING:
                    g.wait_ge(done, t - RING + 1)
                for j in range(2):
                    g.indirect_dma_start(out=y[:, t % RING, j], out_offset=None, in_=core.pad,
                                         in_offset=bass.IndirectOffsetOnAxis(ap=slot[:, j, t:t + 1], axis=0)
                                         ).then_inc(got[t % RING], 16)

        @block.vector
        def _(dve):
            for t in range(NT):
                dve.wait_ge(got[t % RING], 32 * (t // RING + 1))
                nc.vector.scalar_tensor_tensor(h[:, t], y[:, t % RING, 0], wt[:, 0, t:t + 1], h[:, t], ALU.mult,
                                               ALU.add).then_inc(part, 1)
                dve.wait_ge(part, t + 1)
                nc.vector.scalar_tensor_tensor(h[:, t], y[:, t % RING, 1], wt[:, 1, t:t + 1], h[:, t], ALU.mult,
                                               ALU.add).then_inc(done, 1)

        @block.sync
        def _(sp):
            for t in range(NT):
                sp.wait_ge(done, t + 1)
                sp.dma_start(out[0, t * P:(t + 1) * P], h[:, t]).then_inc(stored, 16)
            sp.wait_ge(stored, 16 * NT)


def layer(nc, a, out):
    ctx = ExitStack()
    with ctx:
        core = Core(nc, ctx)
        core.k = Constants()
        core.xt = core.sb("xt", [P, 4, D], R_X[0])
        core.nT = core.sb("nT", [P, KT, S], R_NT[0])
        core.mixed = core.sb("mixed", [P, NT, D], R_MIX[0])
        core.x_in = [core.sem(f"x_in{u}") for u in range(4)]
        ps = ctx.enter_context(nc.psum_tensor("ps", [P, 8 * HALF], F32))
        core.ps = ps
        core.pt = [ps[:, 0:1024], ps[:, 1024:2048]]
        core.wu = [core.sb(f"wu{q}", [P, 2, KT, FF], R_WU[q]) for q in range(NW)]
        core.wd = [core.sb(f"wd{q}", [P, FT, D], R_WD[q]) for q in range(NW)]
        core.wu_in, core.wd_in, core.wu_free, core.wd_free = (
            [core.sem(f"{n}{q}") for q in range(NW)] for n in ("wu_in", "wd_in", "wu_free", "wd_free"))
        core.pad = nc.dram_tensor("pad", (SLOTS + BLK, D), F32, kind="Internal").ap()
        heads = Map(core, *R_WORK)
        core.wt = heads("h_wt", [P, 2, KT, DK])
        core.ww = heads("h_ww", [P, KT, 2 * DK])
        core.wtw_end = heads.at
        core.wt_in, core.ww_in, core.wt_free, core.ww_free = (
            core.sem(n) for n in ("wt_in", "ww_in", "wt_free", "ww_free"))
        ahead = Map(core, *R_WORK)
        core.wq = ahead("a_wq", [P, KT, REP * DH])
        core.wk = ahead("a_wk", [P, KT, 2 * DH])
        core.wc = ahead("a_wc", [P, KT, 2 * DH])
        core.wqkc_end = ahead.at
        core.wq_in, core.wk_in, core.wc_in = core.sem("wq_in"), core.sem("wk_in"), core.sem("wc_in")
        constants(core)
        first_norm(nc, core, a)
        hgrn(nc, core, a)
        attention(nc, core, a)
        out_projection(nc, core, a)
        routing(nc, core, a)
        experts(nc, core, a)
        combine(nc, core, a, out)



def kernel(**inputs):
    import numpy as np
    import concourse.bacc as bacc
    from concourse.bass_utils import run_bass_kernel_spmd

    arrays = {name: np.ascontiguousarray(value) for name, value in inputs.items()}
    nc = bacc.Bacc("TRN2", target_bir_lowering=False, num_devices=1)
    a = {name: nc.dram_tensor(f"in_{name}_dram", value.shape, mybir.dt.from_np(value.dtype), kind="ExternalInput").ap()
         for name, value in arrays.items()}
    out = nc.dram_tensor("out_0", (1, S, D), F32, kind="ExternalOutput").ap()
    layer(nc, a, out)
    nc.finalize()
    feeds = {f"in_{name}_dram": value for name, value in arrays.items()}
    result = run_bass_kernel_spmd(nc, [feeds], core_ids=[0])
    return result.results[0]["out_0"]
```

```python
from contextlib import ExitStack

import concourse.bass as bass
from concourse import mybir
from concourse.alu_op_type import AluOpType as ALU

F32 = mybir.dt.float32
I32 = mybir.dt.int32
U32 = mybir.dt.uint32
U8 = mybir.dt.uint8
ACT = mybir.ActivationFunctionType
AX = mybir.AxisListType

P = 128
S = 1024
D = 1024
NT = S // P
KT = D // P
HALF = 512
EPS = 1e-6
NEG = -1e30

HEADS, GROUPS, DH = 8, 2, 64
REP = HEADS // GROUPS
PAIRS = REP // 2
NSA_W = HEADS * DH
CSTR, CLEN, CHID = 16, 32, 256
NC = S // CSTR - 1
CM = CLEN // 2
WINDOW = 512
HH, DK = 4, 128
HG_W = HH * DK
KV = GROUPS * DH
C_Q, C_KC, C_VC, C_KS, C_VS, C_KW, C_VW = [0] + [NSA_W + i * KV for i in range(6)]
C_GATE = NSA_W + 6 * KV
C_HQ = C_GATE + 3 * HEADS
C_HF, C_HI, C_HG = C_HQ + HG_W, C_HQ + 2 * HG_W, C_HQ + 3 * HG_W
IN_COLS = C_HQ + 4 * HG_W
LEVELS = 7

NG, EPG, NE, FF = 4, 8, 32, 512
BLK = 64
MAXBLK = S * 2 // BLK + NE
SLOTS = MAXBLK * BLK
FT = FF // P


class Chain:

    def __init__(self, eng, sem, per_round=0):
        self.eng, self.sem, self.per_round, self.base, self.n = eng, sem, per_round, 0, 0

    def round(self, i):
        self.base, self.n = i * self.per_round, 0

    def __call__(self, ins):
        self.n += 1
        ins.then_inc(self.sem, 1)

    def wait(self):
        self.eng.wait_ge(self.sem, self.base + self.n)

    def link(self, ins):
        self(ins)
        self.wait()

    def end(self):
        assert self.n == self.per_round, (self.n, self.per_round)


class Core:

    def __init__(self, nc, ctx):
        self.nc, self.ctx = nc, ctx

    def sb(self, name, shape, off, dt=F32):
        return self.nc.alloc_sbuf_tensor_at(name, shape, dt, offset=SB_BASE + off)

    def sem(self, name):
        return self.ctx.enter_context(self.nc.semaphore(name))

    def sems(self, prefix, names):
        return {n: self.sem(prefix + n) for n in names}


class Constants:
    pass


class Map:

    def __init__(self, core, at, end):
        self.core, self.at, self.last = core, at, end

    def __call__(self, name, shape, dt=F32):
        n = {F32: 4, I32: 4, U32: 4, U8: 1}[dt]
        for s in shape[1:]:
            n *= s
        t = self.core.sb(name, shape, self.at, dt)
        self.at += (n + 31) // 32 * 32
        assert self.at <= self.last, (name, self.at, self.last)
        return t


KB = 1024
SB_BASE = 16 * KB + 128
R_CONST = (0, 16 * KB)
R_X = (16 * KB, 48 * KB)
R_MIX = (48 * KB, 80 * KB)
R_NT = (80 * KB, 112 * KB)
R_WORK = (112 * KB, 207 * KB)


def constants(core):
    c = Map(core, *R_CONST)
    k = core.k
    k.ident = c("ident", [P, P])
    k.ones = c("ones", [P, P])
    k.halves = c("halves", [P, P])
    k.before = c("before", [P, P])
    k.causal = c("causal", [P, P])
    k.far = c("far", [P, P])
    k.cmask = c("cmask", [P, NT, NC + 1])
    k.cneg = c("cneg", [P, NT, NC + 1])
    k.lmask = c("lmask", [P, LEVELS, P], U8)
    k.lmaskf = core.sb("lmaskf", [P, LEVELS, P], R_MIX[0])
    k.reset = c("reset", [P, S])
    k.eps = c("eps", [P, 1])
    k.g_hg = c("g_hg", [P, DK])
    k.g_attn = c("g_attn", [P, KT])
    k.g_nsa = c("g_nsa", [P, NSA_W // P])
    k.gq = c("gq", [P, 1])
    k.gkk = c("gkk", [P, 1])
    k.gkc = c("gkc", [P, 1])
    k.lb = c("lb", [P, HH])
    k.oml = c("oml", [P, HH])
    k.lbl = c("lbl", [P, 2, HH])
    k.brt = c("brt", [P, NG + NE])
    k.order = c("order", [P, NE])
    k.wr = c("wr", [P, KT, NG + NE])


def first_norm(nc, core, a):
    k = core.k
    xt, nT = core.xt, core.nT
    x_in = core.x_in
    w = Map(core, R_MIX[0] + 8 * KB, R_MIX[1])
    sq = w("n_sq", [P, D])
    ss = w("n_ss", [P, 4, 2])
    pt = core.pt
    x_sum, x_rs, x_nrm, x_T, x_ev, x_free, c_a = (core.sem(n) for n in (
        "n_sum", "n_rs", "n_scaled", "n_turned", "n_out", "n_free", "n_act"))
    s_ms, s_sel, s_in, g_in, s_a, s_v = (core.sem(n) for n in (
        "const_filled", "const_shaped", "const_in", "gain_in", "const_act", "const_dve"))
    U = 4
    with nc.Block() as block:

        @block.sync
        def _(sp):
            loads = [
                (k.g_nsa[:], a["nsa_out_norm_g"].rearrange("o (t p) -> p (o t)", p=P)),
                (k.gq[0:DH], a["nsa_q_norm_g"].rearrange("o d -> d o")),
                (k.gq[DH:P], a["nsa_q_norm_g"].rearrange("o d -> d o")),
                (k.gkc[0:DH], a["nsa_k_norm_g"][0, 0:1].rearrange("o d -> d o")),
                (k.gkc[DH:P], a["nsa_k_norm_g"][0, 0:1].rearrange("o d -> d o")),
                (k.gkk[0:DH], a["nsa_k_norm_g"][0, 1:2].rearrange("o d -> d o")),
                (k.gkk[DH:P], a["nsa_k_norm_g"][0, 2:3].rearrange("o d -> d o")),
                (k.lbl[:, 0], a["hgrn_lb_logits"][0].rearrange("(h p) -> p h", p=P)),
                (k.lbl[:, 1], a["hgrn_lb_logits"][1].rearrange("(h p) -> p h", p=P)),
                (k.g_hg[:], a["hgrn_out_norm_g"][0].partition_broadcast(P)),
                (k.brt[:, 0:NG], a["moe_b_group"][0].partition_broadcast(P)),
                (k.brt[:, NG:NG + NE], a["moe_b_expert"][0].partition_broadcast(P)),
                (k.wr[:, :, 0:NG], a["moe_w_group"][0].rearrange("(t p) n -> p t n", p=P)),
                (k.wr[:, :, NG:NG + NE], a["moe_w_expert"][0].rearrange("(t p) n -> p t n", p=P)),
            ]
            for u in range(U):
                sp.dma_start(xt[:, u], a["x"][0, u * P:(u + 1) * P]).then_inc(x_in[u], 16)
            with nc.allow_non_contiguous_dma(reason="gains and biases, a few bytes each"):
                sp.dma_start(k.g_attn[:], a["attn_norm_g"].rearrange("o (t p) -> p (o t)", p=P)).then_inc(g_in, 16)
            load_head(sp, core, a, 0)
            for u in range(U):
                sp.wait_ge(x_T, u + 1)
                sp.dma_start(xt[:, u], a["x"][0, (U + u) * P:(U + u + 1) * P]).then_inc(x_in[u], 16)
            with nc.allow_non_contiguous_dma(reason="gains and biases, a few bytes each"):
                for out, src in loads:
                    sp.dma_start(out, src).then_inc(s_in, 16)
            sp.wait_ge(s_in, 16 * len(loads))

        @block.gpsimd
        def _(g):
            sel = []

            def select(out, pattern, op, fill, base, cm):
                if sel:
                    g.wait_ge(s_sel, len(sel))
                sel.append(g.affine_select(out=out, in_=out, pattern=pattern, compare_op=op, fill=fill,
                                           base=base, channel_multiplier=cm).then_inc(s_sel, 1))

            g.memset(k.ident[:], 0.0).then_inc(s_ms, 1)
            g.memset(k.eps[:], EPS).then_inc(s_ms, 1)
            g.wait_ge(s_ms, 2)
            select(k.ident[:], [[-1, P]], ALU.not_equal, 1.0, 0, 1)
            n = 2
            for t, v in ((k.ones, 1.0), (k.halves, 1.0 / DH), (k.before, 1.0),
                         (k.causal, 0.0), (k.far, 0.0), (k.cmask, 1.0), (k.cneg, 0.0),
                         (k.lmaskf, 1.0), (k.reset, 1.0)):
                g.memset(t[:], v).then_inc(s_ms, 1)
                n += 1
            g.wait_ge(s_ms, n)
            select(k.halves[0:DH, DH:P], [[0, DH]], ALU.is_gt, 0.0, 0, 0)
            select(k.halves[DH:P, 0:DH], [[0, DH]], ALU.is_gt, 0.0, 0, 0)
            select(k.before[:], [[1, P]], ALU.is_gt, 0.0, 0, -1)
            select(k.causal[:], [[-1, P]], ALU.is_ge, NEG, 0, 1)
            select(k.far[:], [[1, P]], ALU.is_gt, NEG, 0, -1)
            select(k.cmask[:], [[P, NT], [-CSTR, NC + 1]], ALU.is_ge, 0.0, 1 - CLEN, 1)
            select(k.cneg[:], [[P, NT], [-CSTR, NC + 1]], ALU.is_ge, NEG, 1 - CLEN, 1)
            select(k.reset[:].rearrange("p (c t) -> p c t", t=P), [[0, NT], [1, P]], ALU.is_gt, 0.0, 0, 0)
            for l in range(LEVELS):
                B = 1 << l
                n_blk = P // (2 * B)
                m = k.lmaskf[:, l].rearrange("p (n two b) -> p n two b", two=2, b=B)
                select(m[:, :, 0], [[0, n_blk], [0, B]], ALU.is_gt, 0.0, 0, 0)
                select(m[:, :, 1], [[-2 * B, n_blk], [0, B]], ALU.is_ge, 0.0, 0, 1)
                select(m[:, :, 1], [[2 * B, n_blk], [0, B]], ALU.is_gt, 0.0, B, -1)
            g.wait_ge(s_sel, len(sel))
            g.tensor_copy(k.lmask[:], k.lmaskf[:]).then_inc(s_sel, 1)
            g.wait_ge(s_sel, len(sel) + 1)
            g.iota(k.order[:], pattern=[[-1, NE]], base=NE, channel_multiplier=0,
                   allow_small_or_imprecise_dtypes=True).then_inc(s_sel, 1)
            g.wait_ge(s_sel, len(sel) + 2)

        @block.scalar
        def _(act):
            act.preload_act_table_set("natural_log_exp_and_others")
            c = Chain(act, c_a, 2 * U)
            act.wait_ge(s_ms, 2)
            with act.Fori(0, NT // U) as i:
                c.round(i)
                for u in range(U):
                    act.wait_ge(x_in[u], i * 16 + 16)
                    c.link(nc.scalar.activation(sq[:], xt[:, u], ACT.Square, accum_out=ss[:, u, 0:1]))
                    c.link(nc.scalar.activation(ss[:, u, 0:1], ss[:, u, 0:1], ACT.Ln, scale=1.0 / D, bias=k.eps[:]))
                    nc.scalar.activation(ss[:, u, 1:2], ss[:, u, 0:1], ACT.Exp, scale=-0.5).then_inc(x_rs, 1)
                c.end()
            act.wait_ge(s_v, 3)
            nc.scalar.activation(k.lbl[:], k.lbl[:], ACT.Exp).then_inc(s_a, 1)

        @block.vector
        def _(dve):
            dve.wait_ge(g_in, 16)
            def scale(t):
                dve.wait_ge(x_rs, t + 1)
                nc.vector.tensor_scalar(xt[:, t % U], xt[:, t % U], ss[:, t % U, 1:2], None, ALU.mult).then_inc(x_nrm, 1)

            def take(t):
                dve.wait_ge(x_T, t + 1)
                nc.vector.tensor_tensor(nT[:, :, t * P:(t + 1) * P], pt[t % 2].rearrange("p (k t) -> p k t", t=P),
                                        k.g_attn[:].unsqueeze(2).to_broadcast([P, KT, P]), ALU.mult).then_inc(x_ev, 1)

            scale(0)
            for t in range(NT):
                if t < NT - 1:
                    scale(t + 1)
                take(t)
            c = Chain(dve, s_v)
            dve.wait_ge(s_in, 16 * 14)
            c.link(nc.vector.tensor_max(k.lb[:], k.lbl[:, 0], k.lbl[:, 1]))
            c.link(nc.vector.tensor_sub(k.lbl[:, 0], k.lbl[:, 0], k.lb[:]))
            c.link(nc.vector.tensor_sub(k.lbl[:, 1], k.lbl[:, 1], k.lb[:]))
            dve.wait_ge(s_a, 1)
            c.link(nc.vector.tensor_add(k.oml[:], k.lbl[:, 0], k.lbl[:, 1]))
            c.link(nc.vector.reciprocal(k.oml[:], k.oml[:]))
            c.link(nc.vector.tensor_mul(k.lb[:], k.lbl[:, 0], k.oml[:]))
            c.link(nc.vector.tensor_mul(k.oml[:], k.lbl[:, 1], k.oml[:]))

        @block.tensor
        def _(pe):
            pe.sem_inc(x_ev, 2)
            pe.wait_ge(s_sel, 1)
            with pe.Fori(0, NT // U) as i:
                for u in range(U):
                    pe.wait_ge(x_nrm, i * U + u + 1)
                    pe.wait_ge(x_ev, i * U + u + 1)
                    for kt in range(KT):
                        last = nc.tensor.transpose(pt[u % 2][:, kt * P:(kt + 1) * P], xt[:, u, kt * P:(kt + 1) * P],
                                                   k.ident[:])
                    last.then_inc(x_T, 1)


def load_head(sp, core, a, i):
    win = a["w_in"][0].rearrange("(t p) n -> p t n", p=P)
    if not isinstance(i, int):
        sp.wait_ge(core.wt_free, i)
    for j, col in ((0, C_HQ), (1, C_HF)):
        sp.dma_start(core.wt[:, j], win[:, :, bass.ds(col + i * DK, DK)]).then_inc(core.wt_in, 16)
    if not isinstance(i, int):
        sp.wait_ge(core.ww_free, i)
    for j, col in ((0, C_HI), (1, C_HG)):
        sp.dma_start(core.ww[:, :, j * DK:(j + 1) * DK], win[:, :, bass.ds(col + i * DK, DK)]).then_inc(core.ww_in, 16)


def hgrn(nc, core, a):
    k, nT, mixed, ps = core.k, core.nT, core.mixed, core.ps
    w = Map(core, *R_WORK)
    zero = core.sb("h_zero", [BLK, D], 203 * KB)
    wt, ww = core.wt, core.ww
    w.at = core.wtw_end
    e1 = w("h_e1", [P, S])
    e2 = w("h_e2", [P, S])
    fg = w("h_fg", [P, S])
    lf = w("h_lf", [P, S])
    cum = w("h_cum", [P, S])
    q = w("h_q", [P, S])
    kf = w("h_kf", [P, S])
    qh = w("h_qh", [P, S])
    kh = w("h_kh", [P, S])
    x = Map(core, *R_X)
    dd = [x("h_d0", [P, S]), x("h_d1", [P, S])]
    qe = [x("h_qe0", [P, S]), x("h_qe1", [P, S])]
    ke = [x("h_ke0", [P, S]), x("h_ke1", [P, S])]
    dec = x("h_dec", [P, NT])
    ssq = x("h_ssq", [P, 2, NT])
    vg = w("h_vg", [P, NT, 2 * DK])
    at = w("h_at", [P, NT, P])
    kt_sb = w("h_kt", [P, NT, P])
    st = w("h_st", [P, NT, P])
    og = w("h_og", [P, NT, P])
    gg = w("h_gg", [P, NT, DK])
    TF, TQ = ps[:, 0:2 * HALF], ps[:, 2 * HALF:4 * HALF]
    U, O = TF, TQ
    TOK = [ps[:, 4 * HALF:4 * HALF + 2 * DK], ps[:, 5 * HALF:5 * HALF + 2 * DK]]
    LV = [ps[:, 6 * HALF:7 * HALF], ps[:, 7 * HALF:8 * HALF]]
    names = ("f_ready q_ready o_free tok_ready tok_out mix_done ef eq "
             "fg lf d_ready e_ready lev_ready lv_done lv_out ea dk de kh_ready kt_done kt_out u_half u_done s_half s_ready "
             "merge_go zero_set zeroed o_done osq ossq orstd eg cleared dve").split()
    m = core.sems("h_", names)
    chunks = lambda t: t[:].rearrange("p (c t) -> p c t", t=P)
    with nc.Block() as block:

        @block.sync
        def _(sp):
            with sp.Fori(1, HH) as i:
                load_head(sp, core, a, i)
            sp.wait_ge(core.wt_free, HH)
            load_q(sp, core, a, 0)
            sp.wait_ge(core.ww_free, HH)
            load_keys(sp, core, a, 0)

        @block.gpsimd
        def _(g):
            for t in (*qe, *ke):
                g.memset(t[:], 0.0).then_inc(m["cleared"], 1)
            g.memset(zero[:], 0.0).then_inc(m["zero_set"], 1)
            g.wait_ge(m["zero_set"], 1)
            g.wait_ge(m["q_ready"], 1)
            with g.Fori(0, SLOTS // BLK + 2) as r:
                g.dma_start(core.pad[bass.ts(r, BLK)], zero[:]).then_inc(m["zeroed"], 16)
            g.wait_ge(m["zeroed"], 16 * (SLOTS // BLK + 2))

        @block.tensor
        def _(pe):
            with pe.Fori(0, HH) as i:
                pe.wait_ge(core.wt_in, i * 32 + 32)
                for j, T, free, ready in ((1, TF, m["s_ready"], m["f_ready"]), (0, TQ, m["o_free"], m["q_ready"])):
                    pe.wait_ge(free, i + 1)
                    for half in range(2):
                        for kt in range(KT):
                            last = nc.tensor.matmul(T[:, half * HALF:(half + 1) * HALF], wt[:, j, kt],
                                                    nT[:, kt, half * HALF:(half + 1) * HALF],
                                                    start=kt == 0, stop=kt == KT - 1)
                    last.then_inc(ready, 1)
                pe.wait_ge(core.ww_in, i * 32 + 32)
                for t in range(NT):
                    if t >= 2:
                        pe.wait_ge(m["tok_out"], i * NT + (t - 1))
                    for kt in range(KT):
                        last = nc.tensor.matmul(TOK[t % 2], nT[:, kt, t * P:(t + 1) * P], ww[:, kt],
                                                start=kt == 0, stop=kt == KT - 1)
                        if t == 0 and kt == 0:
                            last.then_inc(core.wt_free, 1)
                    last.then_inc(m["tok_ready"], 1)
                    pe.wait_ge(m["lev_ready"], i * (LEVELS + 1) + t + 1)
                    qs, ks = (q, kf) if t == 0 else (qe[(t - 1) % 2], ke[(t - 1) % 2])
                    for half in range(2):
                        if t > 0:
                            pe.wait_ge(m["lv_out"], i * 16 + (2 * t - 1 + half))
                        for c in range(half * 4, half * 4 + 4):
                            last = nc.tensor.matmul(LV[half][:, (c % 4) * P:(c % 4 + 1) * P], ks[:, c * P:(c + 1) * P],
                                                    qs[:, c * P:(c + 1) * P], start=True, stop=True)
                        last.then_inc(m["lv_done"], 1)
                    if t == 2:
                        pe.wait_ge(m["kh_ready"], i + 1)
                        for c in range(NT):
                            last = nc.tensor.transpose(U[:, c * P:(c + 1) * P], kh[:, c * P:(c + 1) * P], k.ident[:])
                        last.then_inc(m["kt_done"], 1)
                    if t == 5:
                        pe.wait_ge(m["kt_out"], i + 1)
                        pe.wait_ge(m["tok_out"], i * NT + 5)
                        for c in range(4):
                            last = nc.tensor.matmul(U[:, c * P:(c + 1) * P], kt_sb[:, c], vg[:, c, 0:DK],
                                                    start=True, stop=True)
                        last.then_inc(m["u_half"], 1)
                pe.wait_ge(m["tok_out"], i * NT + NT)
                for c in range(4, NT - 1):
                    last = nc.tensor.matmul(U[:, c * P:(c + 1) * P], kt_sb[:, c], vg[:, c, 0:DK],
                                            start=True, stop=True)
                    if c == 4:
                        last.then_inc(core.ww_free, 1)
                last.then_inc(m["u_done"], 1)
                for c in range(NT):
                    if c % 4 == 0:
                        pe.wait_ge(m["lv_out"], i * 16 + 15 + c // 4)
                        pe.wait_ge(m["s_ready"] if c else m["s_half"], i + 1 + c // 4)
                    last = nc.tensor.matmul(O[:, c * P:(c + 1) * P], at[:, c], vg[:, c, 0:DK],
                                            start=True, stop=c == 0)
                    if c:
                        last = nc.tensor.matmul(O[:, c * P:(c + 1) * P], qh[:, c * P:(c + 1) * P], st[:, c],
                                                start=False, stop=True)
                last.then_inc(m["o_done"], 1)

        @block.scalar
        def _(act):
            def tok(i, t):
                act.wait_ge(m["tok_ready"], i * NT + t + 1)
                nc.scalar.copy(vg[:, t], TOK[t % 2]).then_inc(m["tok_out"], 1)

            with act.Fori(0, HH) as i:
                act.wait_ge(m["f_ready"], i + 1)
                nc.scalar.activation(e1[:], TF, ACT.Sigmoid).then_inc(m["ef"], 1)
                act.preload_act_table_set("natural_log_exp_and_others")
                act.wait_ge(m["fg"], i + 1)
                nc.scalar.activation(lf[:], fg[:], ACT.Ln).then_inc(m["lf"], 1)
                act.wait_ge(m["dk"], i + 1)
                nc.scalar.activation(kh[:], kh[:], ACT.Exp).then_inc(m["de"], 1)
                nc.scalar.activation(qh[:], cum[:], ACT.Exp).then_inc(m["ea"], 1)
                nc.scalar.activation(dec[:], chunks(cum)[:, :, P - 1:P], ACT.Exp).then_inc(m["ea"], 1)
                act.wait_ge(m["q_ready"], i + 1)
                nc.scalar.activation(e2[:], TQ, ACT.Sigmoid).then_inc(m["eq"], 1)
                act.preload_act_table_set("natural_log_exp_and_others")
                act.wait_ge(m["mix_done"], i + 1)
                for l in range(LEVELS):
                    act.wait_ge(m["d_ready"], i * LEVELS + l + 1)
                    nc.scalar.activation(dd[l % 2][:], dd[l % 2][:], ACT.Exp).then_inc(m["e_ready"], 1)
                    if l == 0:
                        tok(i, 0)
                    tok(i, l + 1)
                    if l == 2:
                        act.wait_ge(m["kt_done"], i + 1)
                        nc.scalar.copy(kt_sb[:], U.rearrange("p (c t) -> p c t", t=P)).then_inc(m["kt_out"], 1)
                act.wait_ge(m["tok_out"], i * NT + NT)
                nc.scalar.activation(gg[:], vg[:, :, DK:2 * DK], ACT.Sigmoid).then_inc(m["eg"], 1)
                act.preload_act_table_set("natural_log_exp_and_others")
                act.wait_ge(m["o_done"], i + 1)
                nc.scalar.activation(og[:], O.rearrange("p (c t) -> p c t", t=P), ACT.Square).then_inc(m["osq"], 1)
                act.wait_ge(m["ossq"], i + 1)
                nc.scalar.activation(ssq[:, 1], ssq[:, 0], ACT.Ln, scale=1.0 / DK, bias=k.eps[:]).then_inc(m["orstd"], 1)
                act.wait_ge(m["orstd"], i * 2 + 1)
                nc.scalar.activation(ssq[:, 1], ssq[:, 1], ACT.Exp, scale=-0.5).then_inc(m["orstd"], 1)

        @block.vector
        def _(dve):
            c = Chain(dve, m["dve"], 24)

            def halves(l, t):
                return t[:].rearrange("p (n two b) -> p n two b", two=2, b=1 << l)

            def distance(i, l):
                B, n = 1 << l, S >> (l + 1)
                s, d = halves(l, cum), halves(l, dd[l % 2])
                r = s[:, :, 0, B - 1:B].to_broadcast([P, n, B])
                if l >= 2:
                    dve.wait_ge(m["lev_ready"], i * (LEVELS + 1) + l)
                c(nc.vector.tensor_tensor(d[:, :, 0], r, s[:, :, 0], ALU.subtract))
                nc.vector.tensor_tensor(d[:, :, 1], s[:, :, 1], r, ALU.subtract).then_inc(m["d_ready"], 1)

            def merge(i, l):
                for half in range(2):
                    dve.wait_ge(m["lv_done"], i * 16 + (2 * l + half + 1))
                    if l:
                        dve.wait_ge(m["lv_out"], i * 16 + (2 * l - 1 + half))
                    dve.sem_inc(m["merge_go"], 1)
                    src = LV[half].rearrange("p (c t) -> p c t", t=P)
                    dst = at[:, half * 4:half * 4 + 4]
                    if l == 0:
                        nc.vector.tensor_tensor(dst, src, k.ident[:].unsqueeze(1).to_broadcast([P, 4, P]),
                                                ALU.mult).then_inc(m["lv_out"], 1)
                    else:
                        nc.vector.copy_predicated(dst, k.lmask[:, l - 1].unsqueeze(1).to_broadcast([P, 4, P]),
                                                  src).then_inc(m["lv_out"], 1)

            def states(i, half):
                Uc = U.rearrange("p (c t) -> p c t", t=P)
                if half == 0:
                    dve.wait_ge(m["u_half"], i + 1)
                    c.link(nc.vector.tensor_copy(st[:, 1], Uc[:, 0]))
                else:
                    dve.wait_ge(m["u_done"], i + 1)
                    dve.wait_ge(m["s_half"], i + 1)
                for ch in (range(1, 4), range(4, NT - 1))[half]:
                    ins = nc.vector.scalar_tensor_tensor(st[:, ch + 1], st[:, ch], dec[:, ch:ch + 1], Uc[:, ch],
                                                         ALU.mult, ALU.add)
                    if ch == 3:
                        ins.then_inc(m["s_half"], 1)
                    elif ch == NT - 2:
                        ins.then_inc(m["s_ready"], 1)
                    else:
                        c.link(ins)

            dve.sem_inc(m["s_ready"], 1)
            dve.sem_inc(m["o_free"], 1)
            dve.sem_inc(m["mix_done"], 1)
            dve.wait_ge(m["cleared"], 4)
            with dve.Fori(0, HH) as i:
                c.round(i)
                dve.wait_ge(m["ef"], i + 1)
                nc.vector.tensor_scalar(fg[:], e1[:], k.oml[:, bass.ds(i, 1)], k.lb[:, bass.ds(i, 1)], ALU.mult,
                                        ALU.add).then_inc(m["fg"], 1)
                dve.wait_ge(m["fg"], i + 1)
                c.link(nc.vector.tensor_scalar(kf[:], fg[:], -1.0, 1.0, ALU.mult, ALU.add))
                dve.wait_ge(m["lf"], i + 1)
                c.link(nc.vector.tensor_tensor_scan(cum[:], k.reset[:], lf[:], 0.0, ALU.mult, ALU.add))
                nc.vector.tensor_tensor(chunks(kh), chunks(cum)[:, :, P - 1:P].to_broadcast([P, NT, P]), chunks(cum),
                                        ALU.subtract).then_inc(m["dk"], 1)
                distance(i, 0)
                dve.wait_ge(m["de"], i + 1)
                nc.vector.tensor_tensor(kh[:], kh[:], kf[:], ALU.mult).then_inc(m["kh_ready"], 1)
                dve.wait_ge(m["eq"], i + 1)
                nc.vector.tensor_tensor(q[:], TQ, e2[:], ALU.mult).then_inc(m["lev_ready"], 1)
                dve.wait_ge(m["ea"], i * 2 + 2)
                dve.wait_ge(m["lev_ready"], i * (LEVELS + 1) + 1)
                c(nc.vector.tensor_tensor(qh[:], qh[:], q[:], ALU.mult))
                for l in range(LEVELS):
                    if l + 1 < LEVELS:
                        distance(i, l + 1)
                    dve.wait_ge(m["e_ready"], i * LEVELS + l + 1)
                    e = halves(l, dd[l % 2])
                    c(nc.vector.tensor_tensor(halves(l, qe[l % 2])[:, :, 1], halves(l, q)[:, :, 1], e[:, :, 1],
                                              ALU.mult))
                    nc.vector.tensor_tensor(halves(l, ke[l % 2])[:, :, 0], halves(l, kf)[:, :, 0], e[:, :, 0],
                                            ALU.mult).then_inc(m["lev_ready"], 1)
                    merge(i, l)
                    if l == 5:
                        states(i, 0)
                merge(i, LEVELS)
                states(i, 1)
                dve.wait_ge(m["eg"], i + 1)
                c.link(nc.vector.tensor_tensor(gg[:], gg[:], vg[:, :, DK:2 * DK], ALU.mult))
                c.link(nc.vector.tensor_tensor(gg[:], gg[:], k.g_hg[:].unsqueeze(1).to_broadcast([P, NT, DK]),
                                               ALU.mult))
                dve.wait_ge(m["osq"], i + 1)
                nc.vector.tensor_reduce(ssq[:, 0], og[:], AX.X, ALU.add).then_inc(m["ossq"], 1)
                dve.wait_ge(m["orstd"], i * 2 + 2)
                nc.vector.tensor_tensor(og[:], O.rearrange("p (c t) -> p c t", t=P),
                                        ssq[:, 1].unsqueeze(2).to_broadcast([P, NT, P]), ALU.mult).then_inc(m["o_free"], 1)
                dve.wait_ge(m["o_free"], i + 2)
                nc.vector.tensor_tensor(mixed[:, :, bass.ds(NSA_W + i * DK, DK)], og[:], gg[:],
                                        ALU.mult).then_inc(m["mix_done"], 1)
                c.end()


def load_keys(sp, core, a, g):
    win = a["w_in"][0].rearrange("(t p) n -> p t n", p=P)
    for j, col in enumerate((C_KS, C_KW)):
        sp.dma_start(core.wk[:, :, j * DH:(j + 1) * DH],
                     win[:, :, col + g * DH:col + (g + 1) * DH]).then_inc(core.wk_in, 16)
    for j, col in enumerate((C_KC, C_VC)):
        sp.dma_start(core.wc[:, :, j * DH:(j + 1) * DH],
                     win[:, :, col + g * DH:col + (g + 1) * DH]).then_inc(core.wc_in, 16)


def load_q(sp, core, a, g):
    win = a["w_in"][0].rearrange("(t p) n -> p t n", p=P)
    sp.dma_start(core.wq[:], win[:, :, C_Q + g * REP * DH:C_Q + (g + 1) * REP * DH]).then_inc(core.wq_in, 16)


def attention(nc, core, a):
    k, nT, mixed, ps = core.k, core.nT, core.mixed, core.ps
    w = Map(core, *R_WORK)
    x = Map(core, *R_X)
    w1 = [x("a_wk1", [P, CM, CHID]), x("a_wv1", [P, CM, CHID])]
    wq, wk, wc = core.wq, core.wk, core.wc
    w.at = core.wqkc_end
    NG3 = 3 * REP
    VW = 2 * DH + NG3
    wv = w("a_wv", [P, KT, VW])
    wk2 = w("a_wk2", [P, 2, 2, DH])
    wv2 = w("a_wv2", [P, 2, DH])
    pos = w("a_pos", [P, 2, CM])
    gqs = w("a_gqs", [P, 1])
    qT = w("a_qT", [P, PAIRS, S])
    sq = w("a_sq", [P, S])
    rs = w("a_rs", [P, S])
    ksD = w("a_ksD", [P, S])
    kwD = w("a_kwD", [P, S])
    kcD = w("a_kcD", [P, NC])
    vc = w("a_vc", [NC, DH])
    TS = CSTR // 2
    xc = [w("a_xk", [P, 2, S // 2]), w("a_xv", [P, 2, S // 2])]
    sg = w("a_sg", [P, 2, 2, DH])
    hid = w("a_hid", [P, 2, 2, DH])
    vt = w("a_vt", [P, NT, VW])
    pb = [w("a_p0", [P, 2, S]), w("a_p1", [P, 2, S])]
    pT = w("a_pT", [P, 4, HALF])
    nmx = w("a_nmx", [P, 2, 3, 2])
    sums = w("a_sums", [P, 4, 2, 3])
    coef = w("a_coef", [P, 2, 2, 4])
    inv = w("a_inv", [P, 2, 3])
    wo = w("a_wo", [P, 2, 4, DH])
    oT = w("a_oT", [P, 4 * P])
    T3 = [ps[:, j * 2 * HALF:(j + 1) * 2 * HALF] for j in range(4)]
    SC = ps[:, 0:4 * HALF].rearrange("p (h n) -> p h n", h=2)
    PT = [ps[:, 4 * HALF:5 * HALF], ps[:, 5 * HALF:6 * HALF]]
    OT = ps[:, 6 * HALF:7 * HALF]
    OB = ps[:, 7 * HALF:8 * HALF]
    HID = ps[:, 2 * HALF:2 * HALF + 4 * DH].rearrange("p (v h c) -> p v h c", v=2, h=2)
    KC2 = ps[:, 3 * HALF:3 * HALF + NC]
    VC2 = ps[0:NC, 3 * HALF + DH:3 * HALF + 2 * DH]
    VB = [ps[:, 2 * HALF:2 * HALF + VW], ps[:, 3 * HALF:3 * HALF + VW]]

    SEL, WIN, ALL = range(3)
    units = [(p, i, kind) for p in range(PAIRS) for i in range(NT)
             for kind in ((ALL,) if (i + 1) * P < HALF else (SEL, WIN))]
    NU = len(units)
    NV = PAIRS * NT

    def tiles(u):
        _, i, kind = units[u]
        out = [(1, j * P, P, j) for j in range(i + 1)] if kind != WIN else []
        if kind != SEL:
            first, at = max(0, i - WINDOW // P), HALF if kind == ALL else 0
            out += [(2, at + (j - first) * P, P, j) for j in range(first, i + 1)]
            out += [(0, out[-1][1] + P, (CSTR // 2) * i + 7, 0)]
        return out

    def spans(u):
        out = []
        for br, col, n, kt in tiles(u):
            if out and out[-1][0] == br:
                out[-1][2] += n
            else:
                out.append([br, col, n, kt * P])
        return out

    def finished(u):
        return units[u][0] * NT + units[u][1] if 0 <= u < NU and units[u][2] != SEL else None

    chunks, of_unit = [], []
    for u in range(NU):
        mine = []
        t = tiles(u)
        for j in range(0, len(t), 2):
            mine.append(len(chunks))
            chunks.append((u, t[j:j + 2]))
        of_unit.append(mine)
    on_act = set()
    for mine in of_unit:
        on_act.update(mine[::2])
    n_act, n_dve, out_at = 0, 0, []
    for n in range(len(chunks)):
        if n in on_act:
            n_act += 1
            out_at.append(("A", n_act))
        else:
            n_dve += 1
            out_at.append(("D", n_dve))

    names = ("w1_in w2_in wv_in w_free pk_done pc_done pq_done sq_ready n_done n_out rs_ready "
             "normed pc_out v_done v_out hid_done sig hid_ready c2_done kcopy s_done "
             "m_ready p_ready t_done gq_done ptA ptD o_done o_out ot_out o_turned dve ").split()
    m = core.sems("a_", names)
    win = a["w_in"][0].rearrange("(t p) n -> p t n", p=P)

    def out_wait(eng, g, n):
        which, at = out_at[n]
        if which == "A":
            eng.wait_ge(m["ptA"], g * n_act + at)
        else:
            eng.wait_ge(m["ptD"], g * n_dve + at)

    with nc.Block() as block:

        @block.sync
        def _(sp):
            for g in range(GROUPS):
                if g:
                    sp.wait_ge(m["w_free"], g + 1)
                    load_keys(sp, core, a, g)
                    load_q(sp, core, a, g)
                for j, col in enumerate((C_VS, C_VW)):
                    sp.dma_start(wv[:, :, j * DH:(j + 1) * DH],
                                 win[:, :, col + g * DH:col + (g + 1) * DH]).then_inc(m["wv_in"], 16)
                sp.dma_start(wv[:, :, 2 * DH:VW],
                             win[:, :, C_GATE + g * NG3:C_GATE + (g + 1) * NG3]).then_inc(m["wv_in"], 16)

        @block.tensor
        def _(pe):
            def project(out, cols):
                for half in range(2):
                    for kt in range(KT):
                        last = nc.tensor.matmul(out[:, half * HALF:(half + 1) * HALF], cols(kt),
                                                nT[:, kt, half * HALF:(half + 1) * HALF],
                                                start=kt == 0, stop=kt == KT - 1)
                return last

            def squares(out):
                for half in range(2):
                    last = nc.tensor.matmul(out[:, half * HALF:(half + 1) * HALF], k.halves[:],
                                            sq[:, half * HALF:(half + 1) * HALF], start=True, stop=True)
                last.then_inc(m["n_done"], 1)

            def scores(g, u):
                p, i, kind = units[u]
                parts = []
                for br, col, n, key in spans(u):
                    src = (kcD, ksD, kwD)[br]
                    for c in range(0, n, HALF):
                        parts.append((src, key + c, col + c, min(HALF, n - c)))
                for h in range(2):
                    if u:
                        pe.wait_ge(m["p_ready"], g * 2 * NU + 2 * u - 1 + h)
                    r = slice(h * DH, (h + 1) * DH)
                    for src, key, col, n in parts:
                        last = nc.tensor.matmul(SC[:, h, col:col + n], qT[r, p, i * P:(i + 1) * P],
                                                src[r, key:key + n], start=True, stop=True)
                        if u == 0 and col == 0 and h == 0:
                            last.then_inc(m["w_free"], 1)
                    last.then_inc(m["s_done"], 1)

            def turn(g, n):
                u, ts = chunks[n]
                if n >= 2:
                    out_wait(pe, g, n - 2)
                pe.wait_ge(m["p_ready"], g * 2 * NU + 2 * u + 2)
                for j, (_, col, keys, _) in enumerate(ts):
                    for h in range(2):
                        at = (j * 2 + h) * P
                        last = nc.tensor.transpose(PT[n % 2][0:keys, at:at + P], pb[u % 2][:, h, col:col + keys],
                                                   k.ident[:])
                last.then_inc(m["t_done"], 1)

            def values(g, n):
                u, ts = chunks[n]
                p, i, kind = units[u]
                v = p * NT + i
                out_wait(pe, g, n)
                if n == of_unit[u][0] and kind != WIN and v:
                    pe.wait_ge(m["ot_out"], g * NV + v)
                first = max(0, i - WINDOW // P)
                for j, (br, _, keys, kt) in enumerate(ts):
                    p_ = pT[0:keys, n % 4, j * 2 * P:(j + 1) * 2 * P]
                    if br == 1:
                        for odd in ((kt % 2,) if i else (0, 1)):
                            last = nc.tensor.matmul(OT[odd * DH:(odd + 1) * DH, 0:2 * P], vt[:, kt, 0:DH], p_,
                                                    start=kt < 2, stop=kt >= i - 1)
                    elif br == 2:
                        last = nc.tensor.matmul(OT[DH:P, 2 * P:4 * P], vt[:, kt, DH:2 * DH], p_,
                                                start=kt == first, stop=kt == i)
                    else:
                        last = nc.tensor.matmul(OT[0:DH, 2 * P:4 * P], vc[0:keys], p_, start=True, stop=True)
                if kind != SEL and n == of_unit[u][-1]:
                    last.then_inc(m["o_done"], 1)

            def turn_outputs(g, v):
                pe.wait_ge(m["ot_out"], g * NV + v + 1)
                pe.wait_ge(m["o_out"], g * NV + v + 1)
                for h in range(2):
                    for j in range(2):
                        last = nc.tensor.transpose(OB[:, (h * 2 + j) * P:(h * 2 + j + 1) * P],
                                                   oT[:, ((1 - j) * 2 + h) * P:((1 - j) * 2 + h + 1) * P], k.ident[:])
                last.then_inc(m["o_turned"], 1)

            pe.sem_inc(m["w_free"], 1)
            with pe.Fori(0, GROUPS) as g:
                pe.wait_ge(core.wk_in, g * 32 + 32)
                project(T3[0], lambda kt: wk[:, kt]).then_inc(m["pk_done"], 1)
                pe.wait_ge(core.wc_in, g * 32 + 32)
                project(T3[1], lambda kt: wc[:, kt]).then_inc(m["pc_done"], 1)
                pe.wait_ge(core.wq_in, g * 16 + 16)
                project(T3[2], lambda kt: wq[:, kt, 0:P]).then_inc(m["pq_done"], 1)
                pe.wait_ge(m["sq_ready"], g * 4 + 1)
                pe.wait_ge(m["o_out"], g * NV + 1)
                squares(T3[3])
                pe.wait_ge(m["wv_in"], g * 48 + 48)
                pe.wait_ge(m["pc_out"], g * 8 + 8)
                for t in range(NT):
                    if t >= 2:
                        pe.wait_ge(m["v_out"], g * NT + (t - 1))
                    for kt in range(KT):
                        last = nc.tensor.matmul(VB[t % 2], nT[:, kt, t * P:(t + 1) * P], wv[:, kt],
                                                start=kt == 0, stop=kt == KT - 1)
                    last.then_inc(m["v_done"], 1)
                pe.wait_ge(m["sq_ready"], g * 4 + 2)
                pe.wait_ge(m["n_out"], g * 4 + 1)
                squares(T3[3])
                pe.wait_ge(m["normed"], g * 4 + 1)
                project(T3[0], lambda kt: wq[:, kt, P:2 * P]).then_inc(m["pq_done"], 1)
                pe.wait_ge(m["v_out"], g * NT + NT)
                pe.wait_ge(m["w1_in"], 64)
                for kv in range(2):
                    if kv == 1:
                        pe.wait_ge(m["sq_ready"], g * 4 + 3)
                        pe.wait_ge(m["n_out"], g * 4 + 2)
                        squares(T3[3])
                    for half in range(2):
                        for t in range(CM):
                            last = nc.tensor.matmul(HID[:, kv, half, 0:NC], w1[kv][:, t, half * P:(half + 1) * P],
                                                    xc[kv][:, t // TS, t:t + (NC - 1) * TS + 1:TS],
                                                    start=t == 0, stop=t == CM - 1)
                last.then_inc(m["hid_done"], 1)
                pe.wait_ge(m["hid_ready"], g * 4 + 4)
                pe.wait_ge(m["w2_in"], 48)
                for half in range(2):
                    nc.tensor.matmul(KC2, wk2[:, half].rearrange("p a d -> p (a d)"), hid[:, 0, half, 0:NC],
                                     start=half == 0, stop=half == 1)
                for half in range(2):
                    last = nc.tensor.matmul(VC2, hid[:, 1, half, 0:NC], wv2[:, half], start=half == 0, stop=half == 1)
                last.then_inc(m["c2_done"], 1)
                pe.wait_ge(m["sq_ready"], g * 4 + 4)
                pe.wait_ge(m["n_out"], g * 4 + 3)
                nc.tensor.matmul(T3[3][:, 0:NC], k.halves[:], sq[:, 0:NC], start=True, stop=True).then_inc(m["n_done"], 1)
                pe.wait_ge(m["normed"], g * 4 + 4)
                pe.wait_ge(m["kcopy"], g * 3 + 3)
                for u in range(NU + 2):
                    if u < NU:
                        scores(g, u)
                    mine = of_unit[u - 1] if 0 < u <= NU else []
                    for n in mine[:2]:
                        turn(g, n)
                    if finished(u - 2) is not None:
                        turn_outputs(g, finished(u - 2))
                    for n in mine[2:]:
                        turn(g, n)
                        values(g, n - 2)
                    for n in mine[-2:]:
                        values(g, n)

        @block.scalar
        def _(act):
            for kv, name in enumerate(("cmp_wk1", "cmp_wv1")):
                act.dma_start(w1[kv][:], a[name][0].rearrange("(m p) n -> p m n", p=P)).then_inc(m["w1_in"], 16)
            with nc.allow_non_contiguous_dma(reason="positions, 16 numbers of a partition"):
                for kv, name in enumerate(("cmp_pos_k", "cmp_pos_v")):
                    act.dma_start(pos[:, kv], a[name][0].rearrange("(m l) d -> (l d) m", l=2)).then_inc(m["w1_in"], 16)
            for j in range(2):
                act.dma_start(wk2[:, :, j], a["cmp_wk2"][0].rearrange("(h p) d -> p h d", p=P)).then_inc(m["w2_in"], 16)
            act.dma_start(wv2[:], a["cmp_wv2"][0].rearrange("(h p) d -> p h d", p=P)).then_inc(m["w2_in"], 16)

            def out_of(g, n):
                act.wait_ge(m["t_done"], g * len(chunks) + n + 1)
                nk = chunks[n][1][0][2]
                wd = len(chunks[n][1]) * 2 * P
                nc.scalar.copy(pT[0:nk, n % 4, 0:wd], PT[n % 2][0:nk, 0:wd]).then_inc(m["ptA"], 1)

            def outputs(g, v):
                act.wait_ge(m["o_done"], g * NV + v + 1)
                nc.scalar.copy(oT[:], OT).then_inc(m["ot_out"], 1)

            def inverse_norm(g, j, n):
                act.wait_ge(m["n_done"], g * 4 + j + 1)
                if j:
                    act.wait_ge(m["normed"], g * 4 + j)
                nc.scalar.activation(rs[:, 0:n], T3[3][:, 0:n], ACT.Ln, bias=k.eps[:]).then_inc(m["n_out"], 1)
                act.wait_ge(m["n_out"], g * 4 + j + 1)
                nc.scalar.activation(rs[:, 0:n], rs[:, 0:n], ACT.Exp, scale=-0.5).then_inc(m["rs_ready"], 1)

            def v_evac(g, t):
                act.wait_ge(m["v_done"], g * NT + t + 1)
                nc.scalar.copy(vt[:, t], VB[t % 2]).then_inc(m["v_out"], 1)

            with act.Fori(0, GROUPS) as g:
                act.wait_ge(m["pk_done"], g + 1)
                nc.scalar.activation(sq[:], T3[0], ACT.Square).then_inc(m["sq_ready"], 1)
                act.wait_ge(m["pq_done"], g * 2 + 1)
                inverse_norm(g, 0, S)
                nc.scalar.activation(sq[:], T3[2], ACT.Square).then_inc(m["sq_ready"], 1)
                for t in range(NT):
                    v_evac(g, t)
                inverse_norm(g, 1, S)
                act.wait_ge(m["pq_done"], g * 2 + 2)
                nc.scalar.activation(sq[:], T3[0], ACT.Square).then_inc(m["sq_ready"], 1)
                inverse_norm(g, 2, S)
                act.wait_ge(m["v_out"], g * NT + NT)
                nc.scalar.activation(vt[:, :, 2 * DH:VW], vt[:, :, 2 * DH:VW], ACT.Sigmoid).then_inc(m["sig"], 1)
                act.wait_ge(m["hid_done"], g + 1)
                for kv in range(2):
                    for half in range(2):
                        nc.scalar.activation(sg[:, kv, half, 0:NC], HID[:, kv, half, 0:NC], ACT.Sigmoid).then_inc(m["sig"], 1)
                act.preload_act_table_set("natural_log_exp_and_others")
                act.wait_ge(m["c2_done"], g + 1)
                nc.scalar.activation(sq[:, 0:NC], KC2, ACT.Square).then_inc(m["sq_ready"], 1)
                inverse_norm(g, 3, NC)
                for u in range(NU + 2):
                    mine = [n for n in of_unit[u - 1] if n in on_act] if 0 < u <= NU else []
                    if finished(u - 2) is not None:
                        outputs(g, finished(u - 2))
                    if mine:
                        out_of(g, mine.pop(0))
                    if u < NU:
                        p, i, kind = units[u]
                        v = p * NT + i
                        for h in range(2):
                            act.wait_ge(m["m_ready"], g * 2 * NU + 2 * u + h + 1)
                            for br, col, n, _ in spans(u):
                                ins = nc.scalar.activation(pb[u % 2][:, h, col:col + n], SC[:, h, col:col + n],
                                                           ACT.Exp, bias=nmx[:, u % 2, br, h:h + 1],
                                                           accum_out=sums[:, v % 4, h, br:br + 1])
                            ins.then_inc(m["p_ready"], 1)
                            if mine:
                                out_of(g, mine.pop(0))
                    for n in mine:
                        out_of(g, n)

        @block.vector
        def _(dve):
            c = Chain(dve, m["dve"], 195)

            def out_of(g, n):
                dve.wait_ge(m["t_done"], g * len(chunks) + n + 1)
                nk = chunks[n][1][0][2]
                wd = len(chunks[n][1]) * 2 * P
                nc.vector.tensor_copy(pT[0:nk, n % 4, 0:wd], PT[n % 2][0:nk, 0:wd]).then_inc(m["ptD"], 1)

            def mask_and_max(g, u):
                p, i, kind = units[u]
                top = nmx[:, u % 2]
                width, n = min(i + 1, WINDOW // P + 1) * P, (CSTR // 2) * i + 7
                if kind == ALL:
                    dve.wait_ge(m["s_done"], (g * NU + u) * 2 + 2)
                    two = lambda ap, n: ap.unsqueeze(1).to_broadcast([P, 2, n])
                    for at in (0, HALF):
                        d = SC[:, :, at + width - P:at + width]
                        c(nc.vector.tensor_tensor(d, d, two(k.causal[:], P), ALU.add))
                    d = SC[:, :, HALF + width:HALF + width + n]
                    c.link(nc.vector.tensor_tensor(d, d, two(k.cneg[:, i, 0:n], n), ALU.add))
                    c(nc.vector.tensor_reduce(top[:, 0], d, AX.X, ALU.max, negate=True))
                    c(nc.vector.tensor_reduce(top[:, 1], SC[:, :, 0:width], AX.X, ALU.max, negate=True))
                    for h in range(2):
                        nc.vector.tensor_reduce(top[:, 2, h:h + 1], SC[:, h, HALF:HALF + width], AX.X, ALU.max,
                                                negate=True).then_inc(m["m_ready"], 1)
                    return
                if kind == SEL:
                    width = (i + 1) * P
                for h in range(2):
                    dve.wait_ge(m["s_done"], (g * NU + u) * 2 + h + 1)
                    d = SC[:, h, width - P:width]
                    c(nc.vector.tensor_tensor(d, d, k.causal[:], ALU.add))
                    if kind == WIN:
                        if i >= WINDOW // P:
                            d = SC[:, h, 0:P]
                            c(nc.vector.tensor_tensor(d, d, k.far[:], ALU.add))
                        d = SC[:, h, width:width + n]
                        c.link(nc.vector.tensor_tensor(d, d, k.cneg[:, i, 0:n], ALU.add))
                        c(nc.vector.tensor_reduce(top[:, 0, h:h + 1], d, AX.X, ALU.max, negate=True))
                    else:
                        c.wait()
                    nc.vector.tensor_reduce(top[:, 1 + kind, h:h + 1], SC[:, h, 0:width], AX.X, ALU.max,
                                            negate=True).then_inc(m["m_ready"], 1)

            def combine(g, v):
                p, i = v // NT, v % NT
                dve.wait_ge(m["o_turned"], g * NV + v + 1)
                cf = coef[:, v % 2]
                c.link(nc.vector.reciprocal(inv[:], sums[:, v % 4]))
                gates = vt[:, i, 2 * DH + p * 6:2 * DH + p * 6 + 6].rearrange("p (h b) -> p h b", h=2)
                c(nc.vector.tensor_tensor(cf[:, :, 0:2], inv[:, :, 0:3:2], gates[:, :, 0:3:2], ALU.mult))
                both = lambda ap: ap[:, :, 1:2].to_broadcast([P, 2, 2])
                c.link(nc.vector.tensor_tensor(cf[:, :, 2:4], both(inv), both(gates), ALU.mult))
                if i == 0:
                    c(nc.vector.memset(cf[:, :, 3:4], 0.0))
                    c.link(nc.vector.tensor_scalar(cf[:, :, 0:1], cf[:, :, 0:1], k.cmask[:, 0, 0:1], None, ALU.mult))
                flat = wo[:].rearrange("p h b d -> p (h b) d")
                nc.vector.tensor_tensor(flat, OB.rearrange("p (x d) -> p x d", d=DH),
                                        cf.rearrange("p h b -> p (h b)").unsqueeze(2).to_broadcast([P, 8, DH]),
                                        ALU.mult).then_inc(m["o_out"], 1)
                dve.wait_ge(m["o_out"], g * NV + v + 2)
                c.link(nc.vector.tensor_reduce(
                    mixed[:, i, bass.ds(g * REP * DH + p * P, P)].rearrange("p (h d) -> p h d", h=2),
                    wo[:].rearrange("p h b d -> p h d b"), AX.X, ALU.add))

            dve.sem_inc(m["o_out"], 1)
            nc.vector.tensor_scalar(gqs[:], k.gq[:], float(DH) ** -0.5, None, ALU.mult).then_inc(m["gq_done"], 1)
            with dve.Fori(0, GROUPS) as g:
                c.round(g)
                dve.wait_ge(m["pc_done"], g + 1)
                dve.wait_ge(m["w1_in"], 64)
                for kv in range(2):
                    src = T3[1][kv * DH:(kv + 1) * DH].rearrange("p (n two) -> p two n", two=2)
                    for par in range(2):
                        r = slice(par * DH, (par + 1) * DH)
                        for first in range(2):
                            at = pos[r, kv, first * TS:(first + 1) * TS].unsqueeze(1).to_broadcast([DH, S // CSTR, TS])
                            nc.vector.tensor_tensor(xc[kv][r, first].rearrange("p (c t) -> p c t", t=TS),
                                                    src[:, par].rearrange("p (c t) -> p c t", t=TS), at,
                                                    ALU.add).then_inc(m["pc_out"], 1)
                dve.wait_ge(m["rs_ready"], g * 4 + 1)
                lo, hi = slice(0, DH), slice(DH, P)
                c(nc.vector.scalar_tensor_tensor(ksD[lo], T3[0][lo], k.gkk[lo], rs[lo], ALU.mult, ALU.mult))
                nc.vector.scalar_tensor_tensor(kwD[hi], T3[0][hi], k.gkk[hi], rs[hi], ALU.mult,
                                               ALU.mult).then_inc(m["normed"], 1)
                dve.wait_ge(m["normed"], g * 4 + 1)
                nc.vector.tensor_copy(ksD[hi], ksD[lo]).then_inc(m["kcopy"], 1)
                nc.vector.tensor_copy(kwD[lo], kwD[hi]).then_inc(m["kcopy"], 1)
                for j, (src, p) in enumerate(((T3[2], 0), (T3[0], 1))):
                    dve.wait_ge(m["rs_ready"], g * 4 + 2 + j)
                    nc.vector.scalar_tensor_tensor(qT[:, p], src, gqs[:], rs[:], ALU.mult, ALU.mult).then_inc(m["normed"], 1)
                dve.wait_ge(m["sig"], g * 5 + 5)
                for kv in range(2):
                    for half in range(2):
                        nc.vector.tensor_tensor(hid[:, kv, half, 0:NC], HID[:, kv, half, 0:NC],
                                                sg[:, kv, half, 0:NC], ALU.mult).then_inc(m["hid_ready"], 1)
                dve.wait_ge(m["rs_ready"], g * 4 + 4)
                nc.vector.tensor_copy(vc[:], VC2).then_inc(m["kcopy"], 1)
                nc.vector.scalar_tensor_tensor(kcD[:], KC2, k.gkc[:], rs[:, 0:NC], ALU.mult,
                                               ALU.mult).then_inc(m["normed"], 1)
                for u in range(NU + 2):
                    if u < NU:
                        mask_and_max(g, u)
                    if 0 < u <= NU:
                        for n in of_unit[u - 1]:
                            if n not in on_act:
                                out_of(g, n)
                    if finished(u - 2) is not None:
                        combine(g, finished(u - 2))
                c.end()


R_WOUT = (112 * KB, 144 * KB)
R_WU = (144 * KB, 80 * KB, 48 * KB)
R_WD = (176 * KB, 112 * KB, 128 * KB)
NW = 3
R_BLOCK = (1 * KB, 16 * KB)
R_MT = 2 * KB
R_ROUTE = (195 * KB, 196 * KB)
R_TOP = (192 * KB, 207 * KB)


def load_up(sp, core, a, i, q):
    sp.wait_ge(core.wu_free[q], i + 1)
    for j, name in enumerate(("moe_w1", "moe_w3")):
        sp.dma_start(core.wu[q][:, j], a[name][0, bass.ds(i * NW + q, 1)].rearrange("o (p k) f -> p (o k) f", p=P)
                     ).then_inc(core.wu_in[q], 16)


def load_down(sp, core, a, i, q):
    sp.wait_ge(core.wd_free[q], i + 1)
    sp.dma_start(core.wd[q][:], a["moe_w2"][0, bass.ds(i * NW + q, 1)].rearrange("o (j p) d -> p (o j) d", p=P)
                 ).then_inc(core.wd_in[q], 16)


def out_projection(nc, core, a):
    k, ps = core.k, core.ps
    mixed = core.mixed
    mT = core.sb("o_mT", [P, 2, KT, P], R_MT)
    h = core.h = core.sb("o_h", [P, NT, D], R_X[0])
    n2 = core.n2 = core.mixed
    wout = core.sb("o_wout", [P, KT, D], R_WOUT[0])
    t_ = Map(core, *R_TOP)
    lg = core.lg = t_("o_lg", [P, NT, NG + NE])
    ss = t_("o_ss", [P, NT])
    hs = t_("o_hs", [P, NT])
    gf = t_("o_gf", [P, D])
    nT2 = t_("o_nT", [P, KT, P])
    sq = t_("o_sq", [P, D])
    names = ("wout0_in wout1_in gf_in x_in rstd scaled mt_done mtA mtD pr_done added hr n2_ready t_done t_out "
             "lg_done lg_out act").split()
    m = core.sems("o_", names)
    MT = [ps[:, 2 * HALF:3 * HALF], ps[:, 3 * HALF:4 * HALF]]
    H = [ps[:, 4 * HALF:6 * HALF], ps[:, 6 * HALF:8 * HALF]]
    NTB = ps[:, 0:2 * HALF]
    LG = ps[:, 0:NG + NE]
    HT = NT // 2
    with nc.Block() as block:

        @block.sync
        def _(sp):
            for half in range(2):
                cols = slice(half * HALF, (half + 1) * HALF)
                sp.dma_start(wout[:, :, cols],
                             a["w_out"][0].rearrange("(t p) n -> p t n", p=P)[:, :, cols]).then_inc(m[f"wout{half}_in"], 16)
            sp.dma_start(h[:], a["x"][0].rearrange("(t p) d -> p t d", p=P)).then_inc(m["x_in"], 16)
            sp.dma_start(gf[:], a["ffn_norm_g"][0].partition_broadcast(P)).then_inc(m["gf_in"], 16)
            load_up(sp, core, a, 0, 0)
            load_down(sp, core, a, 0, 0)
            load_up(sp, core, a, 0, 1)

        @block.tensor
        def _(pe):
            for q in range(NW):
                pe.sem_inc(core.wu_free[q], 1)
                pe.sem_inc(core.wd_free[q], 1)

            def turn_mixed(t):
                pe.wait_ge(m["scaled"], t + 1)
                if t:
                    pe.wait_ge(m["mtA"], t)
                    pe.wait_ge(m["mtD"], t)
                for kt in range(KT):
                    last = nc.tensor.transpose(MT[kt // 4][:, kt % 4 * P:(kt % 4 + 1) * P],
                                               mixed[:, t, kt * P:(kt + 1) * P], k.ident[:])
                last.then_inc(m["mt_done"], 1)

            def turn_n2(t):
                pe.wait_ge(m["n2_ready"], t + 1)
                if t:
                    pe.wait_ge(m["t_out"], t)
                    pe.wait_ge(m["lg_out"], t)
                for kt in range(KT):
                    last = nc.tensor.transpose(NTB[:, kt * P:(kt + 1) * P], n2[:, t, kt * P:(kt + 1) * P], k.ident[:])
                last.then_inc(m["t_done"], 1)

            def logits(t):
                pe.wait_ge(m["t_out"], t + 1)
                for kt in range(KT):
                    last = nc.tensor.matmul(LG, nT2[:, kt], k.wr[:, kt], start=kt == 0, stop=kt == KT - 1)
                last.then_inc(m["lg_done"], 1)

            def project(t):
                pe.wait_ge(m["mtA"], t + 1)
                pe.wait_ge(m["mtD"], t + 1)
                if t >= 2:
                    pe.wait_ge(m["added"], t - 1)
                for half in range(2):
                    if t == 0:
                        pe.wait_ge(m[f"wout{half}_in"], 16)
                    for kt in range(KT):
                        last = nc.tensor.matmul(H[t % 2][:, half * HALF:(half + 1) * HALF], mT[:, t % 2, kt],
                                                wout[:, kt, half * HALF:(half + 1) * HALF],
                                                start=kt == 0, stop=kt == KT - 1)
                    if half == 0 and t >= 2:
                        logits(t - 2)
                last.then_inc(m["pr_done"], 1)

            turn_mixed(0)
            for t in range(NT):
                if t < NT - 1:
                    turn_mixed(t + 1)
                project(t)
                if t:
                    turn_n2(t - 1)
            logits(NT - 2)
            turn_n2(NT - 1)
            logits(NT - 1)

        @block.scalar
        def _(act):
            c = Chain(act, m["act"])
            for half in range(2):
                for t in range(half * HT, half * HT + HT):
                    c.link(nc.scalar.activation(sq[:, 0:NSA_W], mixed[:, t, 0:NSA_W], ACT.Square,
                                                accum_out=ss[:, t:t + 1]))
                s = ss[:, half * HT:(half + 1) * HT]
                c.link(nc.scalar.activation(s, s, ACT.Ln, scale=1.0 / NSA_W, bias=k.eps[:]))
                nc.scalar.activation(s, s, ACT.Exp, scale=-0.5).then_inc(m["rstd"], 1)

            def mixed_out(t):
                act.wait_ge(m["mt_done"], t + 1)
                if t >= 2:
                    act.wait_ge(m["pr_done"], t - 1)
                nc.scalar.copy(mT[:, t % 2, 4:8].rearrange("p k t -> p (k t)"), MT[1]).then_inc(m["mtA"], 1)

            def n2_out(t):
                act.wait_ge(m["t_done"], t + 1)
                if t:
                    act.wait_ge(m["lg_done"], t)
                nc.scalar.copy(nT2[:].rearrange("p k t -> p (k t)"), NTB).then_inc(m["t_out"], 1)

            mixed_out(0)
            for t in range(NT):
                if t < NT - 1:
                    mixed_out(t + 1)
                act.wait_ge(m["added"], t + 1)
                c.link(nc.scalar.activation(sq[:], h[:, t], ACT.Square, accum_out=hs[:, t:t + 1]))
                c.link(nc.scalar.activation(hs[:, t:t + 1], hs[:, t:t + 1], ACT.Ln, scale=1.0 / D, bias=k.eps[:]))
                nc.scalar.activation(hs[:, t:t + 1], hs[:, t:t + 1], ACT.Exp, scale=-0.5).then_inc(m["hr"], 1)
                if t:
                    n2_out(t - 1)
            n2_out(NT - 1)

        @block.vector
        def _(dve):
            for t in range(NT):
                dve.wait_ge(m["rstd"], t // HT + 1)
                nc.vector.tensor_scalar(mixed[:, t, 0:NSA_W], mixed[:, t, 0:NSA_W], ss[:, t:t + 1], None,
                                        ALU.mult).then_inc(m["scaled"], 1)
            def take_mixed(t):
                dve.wait_ge(m["mt_done"], t + 1)
                if t >= 2:
                    dve.wait_ge(m["pr_done"], t - 1)
                nc.vector.tensor_tensor(mT[:, t % 2, 0:4], MT[0].rearrange("p (k t) -> p k t", t=P),
                                        k.g_nsa[:].unsqueeze(2).to_broadcast([P, NSA_W // P, P]),
                                        ALU.mult).then_inc(m["mtD"], 1)

            def scale(t):
                dve.wait_ge(m["hr"], t + 1)
                nc.vector.scalar_tensor_tensor(n2[:, t], h[:, t], hs[:, t:t + 1], gf[:], ALU.mult,
                                               ALU.mult).then_inc(m["n2_ready"], 1)

            def take_logits(t):
                dve.wait_ge(m["lg_done"], t + 1)
                nc.vector.tensor_tensor(lg[:, t], LG, k.brt[:], ALU.add).then_inc(m["lg_out"], 1)

            take_mixed(0)
            for t in range(NT):
                if t < NT - 1:
                    take_mixed(t + 1)
                if t >= 2:
                    take_logits(t - 2)
                if t == 0:
                    dve.wait_ge(m["x_in"], 16)
                    dve.wait_ge(m["gf_in"], 16)
                dve.wait_ge(m["pr_done"], t + 1)
                nc.vector.tensor_tensor(h[:, t], h[:, t], H[t % 2], ALU.add).then_inc(m["added"], 1)
                scale(t)
            take_logits(NT - 2)
            take_logits(NT - 1)


def routing(nc, core, a):
    k, ps, lg = core.k, core.ps, core.lg
    keep = Map(core, *R_ROUTE)
    wt = core.wtok = keep("r_wt", [P, 2, NT])
    slot = core.slot = keep("r_slot", [P, 2, NT], U32)
    nblk = core.nblk = keep("r_nblk", [P, NE], I32)
    first = core.first = keep("r_first", [P, NE + 2], I32)
    w = Map(core, 196 * KB, 207 * KB + 512)
    EXP = [P, NT, NE]
    gd = w("r_gd", [P, NT, NG])
    ge = w("r_ge", [P, NT, NG])
    go = w("r_go", [P, NT, NG])
    s1 = w("r_s1", [P, NT])
    m12 = w("r_m", [P, 2, NT])
    le = w("r_le", EXP)
    ch = [w("r_c0", EXP), w("r_c1", EXP)]
    cand = w("r_cand", EXP)
    both = w("r_both", EXP)
    off = w("r_off", [P, NT + 1, NE])
    cnt = w("r_cnt", [P, 4, NE])
    ci = w("r_ci", [P, NE], I32)
    RANK = ps[:, 0:NT * NE]
    TOT = ps[:, HALF:HALF + NT * NE]
    m = core.sems("r_", "gexp texp picked ranked slots scattered dve gd_ready t_ready".split())
    with nc.Block() as block:

        @block.sync
        def _(sp):
            load_down(sp, core, a, 0, 1)
            load_down(sp, core, a, 0, 2)

        @block.scalar
        def _(act):
            act.wait_ge(m["gd_ready"], 1)
            nc.scalar.activation(ge[:], gd[:], ACT.Exp).then_inc(m["gexp"], 1)
            act.wait_ge(m["t_ready"], 1)
            nc.scalar.activation(wt[:, 1], wt[:, 1], ACT.Exp).then_inc(m["texp"], 1)

        @block.tensor
        def _(pe):
            pe.wait_ge(m["picked"], 1)
            flat = both[:].rearrange("p t e -> p (t e)")
            nc.tensor.matmul(RANK, k.before[:], flat, start=True, stop=True)
            nc.tensor.matmul(TOT, k.ones[:], flat, start=True, stop=True).then_inc(m["ranked"], 1)

        @block.vector
        def _(dve):
            c = Chain(dve, m["dve"])
            v = nc.vector

            def first_of(out, x, top, order, n):
                wide = lambda ap: ap.unsqueeze(2).to_broadcast([P, NT, n])
                c.link(v.tensor_tensor(out[:], x[:], wide(top), ALU.is_equal))
                c.link(v.tensor_tensor(out[:], out[:], order.unsqueeze(1).to_broadcast([P, NT, n]), ALU.mult))
                c.link(v.tensor_reduce(s1[:], out[:], AX.X, ALU.max))
                c.link(v.tensor_tensor(out[:], out[:], wide(s1[:]), ALU.is_equal))

            gl = lg[:, :, 0:NG]
            c.link(v.tensor_reduce(m12[:, 0], gl, AX.X, ALU.max))
            v.tensor_tensor(gd[:], gl, m12[:, 0].unsqueeze(2).to_broadcast([P, NT, NG]),
                            ALU.subtract).then_inc(m["gd_ready"], 1)
            first_of(go, gl, m12[:, 0], k.order[:, NE - NG:NE], NG)
            le4 = le[:].rearrange("p t (g e) -> p t g e", g=NG)
            wide = lambda ap: ap.unsqueeze(3).to_broadcast([P, NT, NG, EPG])
            c.link(v.tensor_tensor(le4, lg[:, :, NG:NG + NE].rearrange("p t (g e) -> p t g e", g=NG), wide(go[:]), ALU.mult))
            c.link(v.tensor_scalar(go[:], go[:], 1.0, -NEG, ALU.subtract, ALU.mult))
            c.link(v.tensor_tensor(le4, le4, wide(go[:]), ALU.add))
            for j in range(2):
                c.link(v.tensor_reduce(m12[:, j], le[:], AX.X, ALU.max))
                first_of(ch[j], le, m12[:, j], k.order[:], NE)
                if j == 0:
                    c.link(v.scalar_tensor_tensor(le[:], ch[0][:], 2 * NEG, le[:], ALU.mult, ALU.add))
            v.tensor_tensor(both[:], ch[0][:], ch[1][:], ALU.add).then_inc(m["picked"], 1)
            v.tensor_tensor(wt[:, 1], m12[:, 1], m12[:, 0], ALU.subtract).then_inc(m["t_ready"], 1)
            dve.wait_ge(m["gexp"], 1)
            c.link(v.tensor_reduce(s1[:], ge[:], AX.X, ALU.add))
            dve.wait_ge(m["texp"], 1)
            c.link(v.tensor_scalar(wt[:, 0], wt[:, 1], 1.0, None, ALU.add))
            c.link(v.tensor_tensor(s1[:], s1[:], wt[:, 0], ALU.mult))
            c.link(v.reciprocal(wt[:, 0], s1[:]))
            c.link(v.tensor_tensor(wt[:, 1], wt[:, 1], wt[:, 0], ALU.mult))
            dve.wait_ge(m["ranked"], 1)
            c.link(v.memset(off[:, 0], 0.0))
            tot = TOT.rearrange("p (t e) -> p t e", e=NE)
            for t in range(NT):
                c.link(v.tensor_tensor(off[:, t + 1], off[:, t], tot[:, t], ALU.add))
            c.link(v.tensor_scalar(ci[:], off[:, NT], float(BLK - 1), None, ALU.add))
            c.link(v.tensor_scalar(ci[:], ci[:], BLK.bit_length() - 1, None, ALU.arith_shift_right))
            c.link(v.tensor_scalar(cnt[:, 0], ci[:], 1.0, None, ALU.max))
            c(v.tensor_copy(nblk[:], cnt[:, 0]))
            c.link(v.memset(cnt[:, 3], 1.0))
            c.link(v.tensor_tensor_scan(cnt[:, 1], cnt[:, 3], cnt[:, 0], 0.0, ALU.mult, ALU.add))
            c.link(v.tensor_tensor(cnt[:, 2], cnt[:, 1], cnt[:, 0], ALU.subtract))
            c(v.tensor_copy(first[:, 1:NE + 1], cnt[:, 1]))
            c.link(v.tensor_copy(first[:, 0:1], cnt[:, 2, 0:1]))
            c(v.tensor_scalar(first[:, NE + 1:NE + 2], first[:, NE:NE + 1], 1.0, None, ALU.arith_shift_right))
            c.link(v.tensor_scalar(cnt[:, 2], cnt[:, 2], float(BLK), None, ALU.mult))
            c.link(v.tensor_tensor(cand[:], RANK.rearrange("p (t e) -> p t e", e=NE), off[:, 0:NT], ALU.add))
            c.link(v.tensor_tensor(cand[:], cand[:], cnt[:, 2].unsqueeze(1).to_broadcast([P, NT, NE]), ALU.add))
            for j in range(2):
                c.link(v.tensor_tensor(ch[j][:], ch[j][:], cand[:], ALU.mult))
                c.link(v.tensor_reduce(m12[:, j], ch[j][:], AX.X, ALU.add))
                v.tensor_copy(slot[:, j], m12[:, j]).then_inc(m["slots"], 1)

        @block.gpsimd
        def _(g):
            for j in range(2):
                g.wait_ge(m["slots"], j + 1)
                for t in range(NT):
                    g.indirect_dma_start(out=core.pad, out_offset=bass.IndirectOffsetOnAxis(ap=slot[:, j, t:t + 1], axis=0),
                                         in_=core.n2[:, t], in_offset=None).then_inc(m["scattered"], 16)
            g.wait_ge(m["scattered"], 16 * 2 * NT)


def experts(nc, core, a):
    k, ps = core.k, core.ps
    w = Map(core, *R_BLOCK)
    xs = w("m_xs", [BLK, D])
    xb = [core.sb(f"m_xb{r}", [BLK, D], (196 + 4 * r) * KB) for r in range(2)]
    xT = w("m_xT", [P, KT, BLK])
    sil = w("m_sil", [P, FF])
    hb = w("m_h", [P, FF])
    hT = w("m_hT", [P, FT, BLK])
    yb = w("m_y", [P, HALF])
    XT = ps[:, 0:HALF]
    GATE = ps[0:BLK, HALF:2 * HALF]
    UP = ps[BLK:P, HALF:2 * HALF]
    HTB = ps[:, 2 * HALF:2 * HALF + FT * BLK]
    Y = ps[:, 3 * HALF:4 * HALF]
    m = core.sems("m_", "x0_in x1_in x_go x_at xt_done xt_out turn_go u_done silu h_ready ht_done ht_out y_done y_out y_st".split())
    ROUNDS = NE // NW
    nb_of = lambda eng: eng.value_load(core.first[0:1, NE:NE + 1], min_val=NE, max_val=MAXBLK)
    with nc.Block() as block:

        @block.sync
        def _(sp):
            sp.wait_ge(m["x0_in"], 16)
            load_up(sp, core, a, 0, 2)
            with sp.Fori(1, ROUNDS) as i:
                for q in range(NW):
                    load_up(sp, core, a, i, q)
                    load_down(sp, core, a, i, q)
            for q in range(NE % NW):
                load_up(sp, core, a, ROUNDS, q)
                load_down(sp, core, a, ROUNDS, q)

        @block.gpsimd
        def _(g):
            def land(b, r):
                g.dma_start(xb[r][:], core.pad[bass.ds(b * BLK, BLK)]).then_inc(m[f"x{r}_in"], 16)

            def pass_on(j, r, first=False):
                g.wait_ge(m[f"x{r}_in"], j * 16 + 16)
                if not first:
                    g.wait_ge(m["xt_done"], j * 2 + r)
                g.sem_inc(m["x_go"], 1)
                g.tensor_copy(xs[:], xb[r][:]).then_inc(m["x_at"], 1)
                g.wait_ge(m["x_at"], j * 2 + r + 1)

            pairs = g.value_load(core.first[0:1, NE + 1:NE + 2], min_val=NE // 2, max_val=MAXBLK // 2)
            for r in range(2):
                land(r, r)
            for r in range(2):
                pass_on(0, r, r == 0)
                land(2 + r, r)
            with g.Fori(1, pairs) as j:
                for r in range(2):
                    pass_on(j, r)
                    land(j * 2 + 2 + r, r)
            for r in range(2):
                pass_on(pairs, r)

        @block.tensor
        def _(pe):
            def up(b, q, note=None):
                pe.wait_ge(m["xt_out"], b + 1)
                for kt in range(KT):
                    for j, out in enumerate((GATE, UP)):
                        last = nc.tensor.matmul(out, xT[:, kt], core.wu[q][:, j, kt], start=kt == 0, stop=kt == KT - 1)
                        if note is not None and kt == 0 and j == 0:
                            last.then_inc(note, 1)
                last.then_inc(m["u_done"], 1)

            def turn_rows(b):
                pe.wait_ge(m["x_at"], b + 1)
                pe.sem_inc(m["turn_go"], 1)
                rows = xs[:].rearrange("t (p k) -> t k p", k=KT)
                for kt in range(KT):
                    last = nc.tensor.transpose(XT[:, kt * BLK:(kt + 1) * BLK], rows[:, kt], k.ident[0:BLK, 0:BLK])
                last.then_inc(m["xt_done"], 1)

            def down(b, q):
                pe.wait_ge(m["ht_out"], b + 1)
                pe.wait_ge(m["y_out"], b + 1)
                for j in range(FT):
                    for half in range(2):
                        last = nc.tensor.matmul(Y[half * BLK:(half + 1) * BLK], hT[:, j],
                                                core.wd[q][:, j, half * HALF:(half + 1) * HALF],
                                                start=j == 0, stop=j == FT - 1)
                last.then_inc(m["y_done"], 1)

            def turn_hidden(b, note=None):
                pe.wait_ge(m["h_ready"], b + 1)
                pe.sem_inc(m["turn_go"], 1)
                for j in range(FT):
                    last = nc.tensor.transpose(HTB[:, j * BLK:(j + 1) * BLK], hb[BLK:P, j * P:(j + 1) * P],
                                               k.ident[BLK:P, BLK:P])
                    if note is not None and j == 0:
                        last.then_inc(note, 1)
                last.then_inc(m["ht_done"], 1)

            def step(b, q_up, q_down, boundary):
                up(b, q_up, core.wu_free[q_down] if boundary else None)
                turn_rows(b + 1)
                down(b - 1, q_down)
                turn_hidden(b, core.wd_free[q_down] if boundary else None)

            def rest_of(e, q):
                n = pe.value_load(core.nblk[0:1, bass.ds(e, 1)], min_val=1, max_val=S // BLK)
                at = pe.value_load(core.first[0:1, bass.ds(e, 1)], min_val=0, max_val=MAXBLK)
                with pe.If(n > 1):
                    with pe.Fori(at + 1, at + n) as b:
                        step(b, q, q, False)
                return pe.value_load(core.first[0:1, bass.ds(e + 1, 1)], min_val=1, max_val=MAXBLK)

            turn_rows(0)
            pe.wait_ge(core.wu_in[0], 32)
            up(0, 0)
            turn_rows(1)
            turn_hidden(0)
            def one(i, q):
                nq = (q + 1) % NW
                pe.wait_ge(core.wd_in[q], i * 16 + 16)
                nxt = rest_of(i * NW + q, q)
                pe.wait_ge(core.wu_in[nq], i * 32 + (32 if nq else 64))
                step(nxt, nq, q, True)

            with pe.Fori(0, ROUNDS) as i:
                for q in range(NW):
                    one(i, q)
            one(ROUNDS, 0)
            pe.wait_ge(core.wd_in[1], ROUNDS * 16 + 16)
            nb = rest_of(NE - 1, 1)
            down(nb - 1, 1)

        @block.scalar
        def _(act):
            def silu(b):
                act.wait_ge(m["u_done"], b + 1)
                nc.scalar.activation(sil[BLK:P], GATE, ACT.Silu).then_inc(m["silu"], 1)

            def take(b):
                act.wait_ge(m["y_done"], b + 1)
                act.wait_ge(m["y_st"], b * 32 + 32)
                nc.scalar.copy(yb[:], Y).then_inc(m["y_out"], 1)
                act.wait_ge(m["y_out"], b + 2)
                for half in range(2):
                    act.dma_start(core.pad[bass.ds(b * BLK, BLK), half * HALF:(half + 1) * HALF],
                                  yb[half * BLK:(half + 1) * BLK]).then_inc(m["y_st"], 16)

            act.sem_inc(m["y_out"], 1)
            act.sem_inc(m["y_st"], 32)
            nb = nb_of(act)
            silu(0)
            with act.Fori(1, nb) as b:
                silu(b)
                take(b - 1)
            take(nb - 1)

        @block.vector
        def _(dve):
            def take_rows(b):
                dve.wait_ge(m["xt_done"], b + 1)
                nc.vector.tensor_copy(xT[:].rearrange("p k t -> p (k t)"), XT).then_inc(m["xt_out"], 1)

            nb = nb_of(dve)
            take_rows(0)
            with dve.Fori(0, nb) as b:
                take_rows(b + 1)
                dve.wait_ge(m["silu"], b + 1)
                nc.vector.tensor_tensor(hb[BLK:P], sil[BLK:P], UP, ALU.mult).then_inc(m["h_ready"], 1)
                dve.wait_ge(m["ht_done"], b + 1)
                nc.vector.tensor_copy(hT[:].rearrange("p j t -> p (j t)"), HTB).then_inc(m["ht_out"], 1)
    core.m_y_st, core.nb_of = m["y_st"], nb_of


def combine(nc, core, a, out):
    h, wt, slot = core.h, core.wtok, core.slot
    RING = 4
    y = core.sb("c_y", [P, RING, 2, D], R_MIX[0])
    got = [core.sem(f"c_got{r}") for r in range(RING)]
    part, done, stored = core.sem("c_part"), core.sem("c_done"), core.sem("c_stored")
    go = core.sem("c_go")
    with nc.Block() as block:

        @block.gpsimd
        def _(g):
            nb = core.nb_of(g)
            g.wait_ge(core.m_y_st, nb * 32 + 32)
            g.sem_inc(go, 1)
            for t in range(NT):
                if t >= RING:
                    g.wait_ge(done, t - RING + 1)
                for j in range(2):
                    g.indirect_dma_start(out=y[:, t % RING, j], out_offset=None, in_=core.pad,
                                         in_offset=bass.IndirectOffsetOnAxis(ap=slot[:, j, t:t + 1], axis=0)
                                         ).then_inc(got[t % RING], 16)

        @block.vector
        def _(dve):
            for t in range(NT):
                dve.wait_ge(got[t % RING], 32 * (t // RING + 1))
                nc.vector.scalar_tensor_tensor(h[:, t], y[:, t % RING, 0], wt[:, 0, t:t + 1], h[:, t], ALU.mult,
                                               ALU.add).then_inc(part, 1)
                dve.wait_ge(part, t + 1)
                nc.vector.scalar_tensor_tensor(h[:, t], y[:, t % RING, 1], wt[:, 1, t:t + 1], h[:, t], ALU.mult,
                                               ALU.add).then_inc(done, 1)

        @block.sync
        def _(sp):
            for t in range(NT):
                sp.wait_ge(done, t + 1)
                sp.dma_start(out[0, t * P:(t + 1) * P], h[:, t]).then_inc(stored, 16)
            sp.wait_ge(stored, 16 * NT)


def layer(nc, a, out):
    ctx = ExitStack()
    with ctx:
        core = Core(nc, ctx)
        core.k = Constants()
        core.xt = core.sb("xt", [P, 4, D], R_X[0])
        core.nT = core.sb("nT", [P, KT, S], R_NT[0])
        core.mixed = core.sb("mixed", [P, NT, D], R_MIX[0])
        core.x_in = [core.sem(f"x_in{u}") for u in range(4)]
        ps = ctx.enter_context(nc.psum_tensor("ps", [P, 8 * HALF], F32))
        core.ps = ps
        core.pt = [ps[:, 0:1024], ps[:, 1024:2048]]
        core.wu = [core.sb(f"wu{q}", [P, 2, KT, FF], R_WU[q]) for q in range(NW)]
        core.wd = [core.sb(f"wd{q}", [P, FT, D], R_WD[q]) for q in range(NW)]
        core.wu_in, core.wd_in, core.wu_free, core.wd_free = (
            [core.sem(f"{n}{q}") for q in range(NW)] for n in ("wu_in", "wd_in", "wu_free", "wd_free"))
        core.pad = nc.dram_tensor("pad", (SLOTS + 2 * BLK, D), F32, kind="Internal").ap()
        heads = Map(core, *R_WORK)
        core.wt = heads("h_wt", [P, 2, KT, DK])
        core.ww = heads("h_ww", [P, KT, 2 * DK])
        core.wtw_end = heads.at
        core.wt_in, core.ww_in, core.wt_free, core.ww_free = (
            core.sem(n) for n in ("wt_in", "ww_in", "wt_free", "ww_free"))
        ahead = Map(core, *R_WORK)
        core.wq = ahead("a_wq", [P, KT, REP * DH])
        core.wk = ahead("a_wk", [P, KT, 2 * DH])
        core.wc = ahead("a_wc", [P, KT, 2 * DH])
        core.wqkc_end = ahead.at
        core.wq_in, core.wk_in, core.wc_in = core.sem("wq_in"), core.sem("wk_in"), core.sem("wc_in")
        constants(core)
        first_norm(nc, core, a)
        hgrn(nc, core, a)
        attention(nc, core, a)
        out_projection(nc, core, a)
        routing(nc, core, a)
        experts(nc, core, a)
        combine(nc, core, a, out)



def kernel(**inputs):
    import numpy as np
    import concourse.bacc as bacc
    from concourse.bass_utils import run_bass_kernel_spmd

    arrays = {name: np.ascontiguousarray(value) for name, value in inputs.items()}
    nc = bacc.Bacc("TRN2", target_bir_lowering=False, num_devices=1)
    a = {name: nc.dram_tensor(f"in_{name}_dram", value.shape, mybir.dt.from_np(value.dtype), kind="ExternalInput").ap()
         for name, value in arrays.items()}
    out = nc.dram_tensor("out_0", (1, S, D), F32, kind="ExternalOutput").ap()
    layer(nc, a, out)
    nc.finalize()
    feeds = {f"in_{name}_dram": value for name, value in arrays.items()}
    result = run_bass_kernel_spmd(nc, [feeds], core_ids=[0])
    return result.results[0]["out_0"]
```
